# Optimizing a Trainium2 kernel written in Bass

```python
import math
import jax, jax.numpy as jnp
from jax import lax
import numpy as np

D_MODEL = 1024
BATCH = 1
SEQ = 512
DEPTH = 1

SSM_GROUP = 16
SSM_WIDTH = D_MODEL // 2
SSM_GROUPS = SSM_WIDTH // SSM_GROUP
SSM_STATE = 64
CONV_WIDTH = D_MODEL
CONV_K = 3
D_FF = 4 * D_MODEL
NORM_EPS = 1e-6
DT_MIN = 1e-3
DT_MAX = 1e-1
SPLIT_SIZES = (SSM_WIDTH, CONV_WIDTH, CONV_WIDTH, CONV_WIDTH, D_MODEL, D_MODEL)
IN_COLS = sum(SPLIT_SIZES)
SPLIT_POINTS = tuple(int(v) for v in np.cumsum(SPLIT_SIZES)[:-1])


def rmsnorm(x, g):
    xf = x.astype(jnp.float32)
    var = jnp.mean(xf * xf, axis=-1, keepdims=True)
    return (xf * lax.rsqrt(var + NORM_EPS) * g.astype(jnp.float32)).astype(x.dtype)

def _ssm_combine(e1, e2):
    a1r, a1i, b1r, b1i = e1
    a2r, a2i, b2r, b2i = e2
    ar = a1r * a2r - a1i * a2i
    ai = a1r * a2i + a1i * a2r
    br = a2r * b1r - a2i * b1i + b2r
    bi = a2r * b1i + a2i * b1r + b2i
    return (ar, ai, br, bi)

def s5_branch(u, lam_re, lam_im, log_dt, b_re, b_im, c_re, c_im, d_skip):
    f32 = jnp.float32
    bsz, seq, _ = u.shape
    uf = u.astype(f32).reshape(bsz, seq, SSM_GROUPS, SSM_GROUP)
    lr = lam_re.astype(f32)
    li = lam_im.astype(f32)
    dt = jnp.exp(log_dt.astype(f32))[:, None]
    mag = jnp.exp(lr * dt)
    ab_re = mag * jnp.cos(li * dt)
    ab_im = mag * jnp.sin(li * dt)
    er = ab_re - 1.0
    ei = ab_im
    den = lr * lr + li * li
    q_re = (er * lr + ei * li) / den
    q_im = (ei * lr - er * li) / den
    br = b_re.astype(f32)
    bi = b_im.astype(f32)
    bb_re = q_re[..., None] * br - q_im[..., None] * bi
    bb_im = q_re[..., None] * bi + q_im[..., None] * br
    bu_re = jnp.einsum('gnc,bsgc->bsgn', bb_re, uf)
    bu_im = jnp.einsum('gnc,bsgc->bsgn', bb_im, uf)
    a_re = jnp.broadcast_to(ab_re[None, None], (1, seq, SSM_GROUPS, SSM_STATE))
    a_im = jnp.broadcast_to(ab_im[None, None], (1, seq, SSM_GROUPS, SSM_STATE))
    _, _, s_re, s_im = lax.associative_scan(_ssm_combine, (a_re, a_im, bu_re, bu_im), axis=1)
    y = (jnp.einsum('gcn,bsgn->bsgc', c_re.astype(f32), s_re)
         - jnp.einsum('gcn,bsgn->bsgc', c_im.astype(f32), s_im))
    y = y + d_skip.astype(f32).reshape(SSM_GROUPS, SSM_GROUP) * uf
    return y.reshape(bsz, seq, SSM_WIDTH)

def causal_short_conv(v, w, b):
    seq = v.shape[1]
    vp = jnp.pad(v, ((0, 0), (CONV_K - 1, 0), (0, 0)))
    out = b
    for k in range(CONV_K):
        out = out + w[k] * vp[:, k:k + seq]
    return out

def mixer_block(xn, w_in, b_in, lam_re, lam_im, log_dt, b_re, b_im, c_re, c_im, d_skip,
                w_glu_a, w_glu_b, conv_w, conv_b, w_conv_out, w_out):
    proj = jnp.einsum('bsd,de->bse', xn, w_in) + b_in
    u_ssm, c_bgate, c_cgate, c_val, g_ssm, g_conv = jnp.split(proj, SPLIT_POINTS, axis=-1)
    y_ssm = s5_branch(u_ssm, lam_re, lam_im, log_dt, b_re, b_im, c_re, c_im, d_skip).astype(xn.dtype)
    z = jax.nn.gelu(y_ssm)
    y_a = jnp.einsum('bse,ed->bsd', z, w_glu_a) * jax.nn.sigmoid(jnp.einsum('bse,ed->bsd', z, w_glu_b))
    y_b = jnp.einsum('bse,ed->bsd', c_bgate * causal_short_conv(c_cgate * c_val, conv_w, conv_b), w_conv_out)
    merged = jax.nn.sigmoid(g_ssm) * y_a + jax.nn.sigmoid(g_conv) * y_b
    return jnp.einsum('bsd,de->bse', merged, w_out)

def squared_relu_mlp(xn, w_ff1, w_ff2):
    h = jax.nn.relu(jnp.einsum('bsd,df->bsf', xn, w_ff1))
    return jnp.einsum('bsf,fd->bsd', h * h, w_ff2)

def first_inputs(seed: int = 0) -> dict:
    key = jax.random.key(seed)
    ks = jax.random.split(key, 24)
    L, D, G, N, C = DEPTH, D_MODEL, SSM_GROUPS, SSM_STATE, SSM_GROUP
    nrm = jax.random.normal
    x = nrm(ks[0], (BATCH, SEQ, D), jnp.float32)
    norm_mix_g = 1.0 + 0.02 * nrm(ks[1], (L, D), jnp.float32)
    w_in = nrm(ks[2], (L, D, IN_COLS), jnp.float32) * D ** -0.5
    b_in = 0.02 * nrm(ks[3], (L, IN_COLS), jnp.float32)
    n_idx = jnp.arange(N, dtype=jnp.float32)
    lam_re = -0.5 + 0.01 * nrm(ks[4], (L, G, N), jnp.float32)
    lam_im = math.pi * n_idx[None, None, :] + 0.01 * nrm(ks[5], (L, G, N), jnp.float32)
    log_dt = jax.random.uniform(ks[6], (L, G), jnp.float32, math.log(DT_MIN), math.log(DT_MAX))
    ssm_b_re = nrm(ks[7], (L, G, N, C), jnp.float32) * (2.0 * C) ** -0.5
    ssm_b_im = nrm(ks[8], (L, G, N, C), jnp.float32) * (2.0 * C) ** -0.5
    ssm_c_re = nrm(ks[9], (L, G, C, N), jnp.float32) * (2.0 * N) ** -0.5
    ssm_c_im = nrm(ks[10], (L, G, C, N), jnp.float32) * (2.0 * N) ** -0.5
    ssm_d = 1.0 + 0.1 * nrm(ks[11], (L, SSM_WIDTH), jnp.float32)
    w_glu_a = nrm(ks[12], (L, SSM_WIDTH, D), jnp.float32) * SSM_WIDTH ** -0.5
    w_glu_b = nrm(ks[13], (L, SSM_WIDTH, D), jnp.float32) * SSM_WIDTH ** -0.5
    conv_w = nrm(ks[14], (L, CONV_K, CONV_WIDTH), jnp.float32) * CONV_K ** -0.5
    conv_b = 0.02 * nrm(ks[15], (L, CONV_WIDTH), jnp.float32)
    w_conv_out = nrm(ks[16], (L, CONV_WIDTH, D), jnp.float32) * CONV_WIDTH ** -0.5
    w_out = nrm(ks[17], (L, D, D), jnp.float32) * D ** -0.5
    norm_mlp_g = 1.0 + 0.02 * nrm(ks[18], (L, D), jnp.float32)
    w_ff1 = nrm(ks[19], (L, D, D_FF), jnp.float32) * D ** -0.5
    w_ff2 = nrm(ks[20], (L, D_FF, D), jnp.float32) * D_FF ** -0.5
    norm_final_g = 1.0 + 0.02 * nrm(ks[21], (D,), jnp.float32)
    return {"x": x, "norm_mix_g": norm_mix_g, "w_in": w_in, "b_in": b_in,
            "lam_re": lam_re, "lam_im": lam_im, "log_dt": log_dt,
            "ssm_b_re": ssm_b_re, "ssm_b_im": ssm_b_im, "ssm_c_re": ssm_c_re, "ssm_c_im": ssm_c_im,
            "ssm_d": ssm_d, "w_glu_a": w_glu_a, "w_glu_b": w_glu_b,
            "conv_w": conv_w, "conv_b": conv_b, "w_conv_out": w_conv_out, "w_out": w_out,
            "norm_mlp_g": norm_mlp_g, "w_ff1": w_ff1, "w_ff2": w_ff2, "norm_final_g": norm_final_g}

def first_block(x, norm_mix_g, w_in, b_in, lam_re, lam_im, log_dt, ssm_b_re, ssm_b_im, ssm_c_re, ssm_c_im,
              ssm_d, w_glu_a, w_glu_b, conv_w, conv_b, w_conv_out, w_out, norm_mlp_g, w_ff1, w_ff2,
              norm_final_g):
    h = x
    for l in range(DEPTH):
        xn = rmsnorm(h, norm_mix_g[l])
        h = h + mixer_block(xn, w_in[l], b_in[l], lam_re[l], lam_im[l], log_dt[l],
                            ssm_b_re[l], ssm_b_im[l], ssm_c_re[l], ssm_c_im[l], ssm_d[l],
                            w_glu_a[l], w_glu_b[l], conv_w[l], conv_b[l], w_conv_out[l], w_out[l])
        xn = rmsnorm(h, norm_mlp_g[l])
        h = h + squared_relu_mlp(xn, w_ff1[l], w_ff2[l])
    return rmsnorm(h, norm_final_g)


CTX_LEN = 256
GRID_W = 64
MIX_W = D_MODEL
F_W = MIX_W // 2
F_GROUPS = 4
F_GROUP_W = F_W // F_GROUPS
DN_W = MIX_W - F_W
DN_HEADS = 4
DK = DN_W // DN_HEADS
DV = DN_W // DN_HEADS
QK_W = DN_HEADS * DK
V_W = DN_HEADS * DV
CONV_CH = 2 * QK_W + V_W
W_IN = F_W + CONV_CH + V_W + 4 * DN_HEADS
CHUNK = 64
N_GROUPS = 4
EXPERTS_PER_GROUP = 8
N_EXPERTS = N_GROUPS * EXPERTS_PER_GROUP
TOP_K = 2
D_EXPERT = D_MODEL // 2
MOE_BLOCK = 128
EPS = 1e-6


def rmsnorm_2(x, g):
    xf = x.astype(jnp.float32)
    y = xf * lax.rsqrt(jnp.mean(xf * xf, axis=-1, keepdims=True) + EPS) * g.astype(jnp.float32)
    return y.astype(x.dtype)

def l2norm(a):
    af = a.astype(jnp.float32)
    return af * lax.rsqrt(jnp.sum(af * af, axis=-1, keepdims=True) + EPS)

def modulate(h, shift, scale):
    return h * (1 + scale) + shift

def conv_grid(u, w):
    b, t, ch = u.shape
    rows = t // GRID_W
    y = lax.conv_general_dilated(u.reshape(b, rows, GRID_W, ch), w[:, :, None, :].astype(u.dtype),
                                 (1, 1), 'SAME', dimension_numbers=('NHWC', 'HWIO', 'NHWC'),
                                 feature_group_count=ch)
    return y.reshape(b, t, ch)

def conv_seq(u, w):
    ch = u.shape[-1]
    return lax.conv_general_dilated(u, w[1][:, None, :].astype(u.dtype), (1,), 'SAME',
                                    dimension_numbers=('NWC', 'WIO', 'NWC'), feature_group_count=ch)

def fourier_mix(f):
    b, t, _ = f.shape
    fg = f.astype(jnp.float32).reshape(b, t, F_GROUPS, F_GROUP_W)
    out = jnp.fft.fft2(fg, axes=(1, 3), norm='ortho').real
    return out.reshape(b, t, F_W).astype(f.dtype)

def gated_delta_chunked(q, k, v, g, beta, s0):
    b, t, h, dk = q.shape
    dv = v.shape[-1]
    n = t // CHUNK

    def chunks(a):
        a = jnp.moveaxis(a.astype(jnp.float32), 2, 1)
        return a.reshape(b, h, n, CHUNK, *a.shape[3:])

    q = chunks(q) * dk ** -0.5
    k = chunks(k)
    v = chunks(v)
    beta = chunks(beta)
    gc = jnp.cumsum(chunks(g), axis=-1)
    idx = jnp.arange(CHUNK)
    lower = idx[:, None] >= idx[None, :]
    decay = jnp.exp(jnp.where(lower, gc[..., :, None] - gc[..., None, :], -jnp.inf))
    k_beta = k * beta[..., None]
    m = jnp.where(idx[:, None] > idx[None, :],
                  jnp.einsum('bhnid,bhnjd->bhnij', k_beta, k) * decay, 0.0)
    eye = jnp.eye(CHUNK, dtype=jnp.float32)
    a_mat = eye + m
    t_inv = lax.linalg.triangular_solve(a_mat, jnp.broadcast_to(eye, a_mat.shape), left_side=True,
                                        lower=True, unit_diagonal=True)
    u = t_inv @ (v * beta[..., None])
    w = t_inv @ (k_beta * jnp.exp(gc)[..., None])
    intra = jnp.einsum('bhnid,bhnjd->bhnij', q, k) * decay

    def step(s, blk):
        q_i, k_i, u_i, w_i, a_i, g_i = blk
        v_new = u_i - w_i @ s
        o_i = (q_i * jnp.exp(g_i)[..., None]) @ s + a_i @ v_new
        g_last = g_i[..., -1:]
        s = s * jnp.exp(g_last)[..., None] + jnp.einsum(
            'bhcd,bhce->bhde', k_i * jnp.exp(g_last - g_i)[..., None], v_new)
        return s, o_i

    xs = tuple(jnp.moveaxis(a, 2, 0) for a in (q, k, u, w, intra, gc))
    s_final, o = lax.scan(step, s0.astype(jnp.float32), xs)
    o = jnp.moveaxis(o, 0, 2).reshape(b, h, t, dv)
    return jnp.moveaxis(o, 1, 2), s_final

def bidir_delta(q, k, v, g, beta, s0_fwd, s0_bwd):
    flip = lambda a: jnp.flip(a, axis=1)
    o_f, s_f = gated_delta_chunked(q, k, v, g[:, :, 0], beta[:, :, 0], s0_fwd)
    o_b, s_b = gated_delta_chunked(flip(q), flip(k), flip(v), flip(g[:, :, 1]), flip(beta[:, :, 1]), s0_bwd)
    return o_f + flip(o_b), s_f, s_b

def mixer_features(h, w_in, conv_w, a_log, dt_bias, conv_fn):
    b, t = h.shape[:2]
    p = h @ w_in
    f, qkv, z, gates = jnp.split(p, [F_W, F_W + CONV_CH, F_W + CONV_CH + V_W], axis=-1)
    qkv = jax.nn.silu(conv_fn(qkv, conv_w))
    q, k, v = jnp.split(qkv, [QK_W, 2 * QK_W], axis=-1)
    q = l2norm(q.reshape(b, t, DN_HEADS, DK))
    k = l2norm(k.reshape(b, t, DN_HEADS, DK))
    v = v.reshape(b, t, DN_HEADS, DV)
    gates = gates.astype(jnp.float32).reshape(b, t, 2, 2, DN_HEADS)
    beta = jax.nn.sigmoid(gates[:, :, 0])
    g = -jnp.exp(a_log.astype(jnp.float32)) * jax.nn.softplus(gates[:, :, 1] + dt_bias.astype(jnp.float32))
    return f, q, k, v, z, g, beta

def mixer_output(f, o, z, onorm_g, w_out):
    b, t = f.shape[:2]
    o = (rmsnorm_2(o, onorm_g) * jax.nn.silu(z.reshape(b, t, DN_HEADS, DV))).astype(f.dtype)
    return jnp.concatenate([fourier_mix(f), o.reshape(b, t, V_W)], axis=-1) @ w_out

def moe_ffn(h, w_group, b_group, w_router, b_router, w_gate, w_up, w_down):
    shp = h.shape
    d = shp[-1]
    xf = h.reshape(-1, d)
    n = xf.shape[0]
    pg = jax.nn.softmax((xf @ w_group).astype(jnp.float32) + b_group.astype(jnp.float32), axis=-1)
    pg_top, g_top = lax.top_k(pg, 1)
    el = ((xf @ w_router).astype(jnp.float32) + b_router.astype(jnp.float32)).reshape(
        n, N_GROUPS, EXPERTS_PER_GROUP)
    el_g = el[jnp.arange(n), g_top[:, 0]]
    pe_top, e_top = lax.top_k(jax.nn.softmax(el_g, axis=-1), TOP_K)
    wts = pg_top * pe_top / jnp.sum(pe_top, axis=-1, keepdims=True)
    eid = (g_top * EXPERTS_PER_GROUP + e_top).reshape(-1).astype(jnp.int32)
    w_f = wts.reshape(-1)
    n_assign = n * TOP_K
    order = jnp.argsort(eid)
    e_s = eid[order]
    tok_s = (order // TOP_K).astype(jnp.int32)
    w_s = w_f[order]
    counts = jnp.zeros((N_EXPERTS,), jnp.int32).at[eid].add(1)
    start = jnp.cumsum(counts) - counts
    pcounts = (counts + MOE_BLOCK - 1) // MOE_BLOCK * MOE_BLOCK
    pend = jnp.cumsum(pcounts)
    pstart = pend - pcounts
    dest = pstart[e_s] + (jnp.arange(n_assign, dtype=jnp.int32) - start[e_s])
    n_slots = -(-n_assign // MOE_BLOCK) * MOE_BLOCK + N_EXPERTS * MOE_BLOCK
    n_blocks = n_slots // MOE_BLOCK
    slot_tok = jnp.full((n_slots,), n, jnp.int32).at[dest].set(tok_s)
    slot_w = jnp.zeros((n_slots,), jnp.float32).at[dest].set(w_s)
    blk_expert = jnp.minimum(
        jnp.searchsorted(pend, jnp.arange(n_blocks, dtype=jnp.int32) * MOE_BLOCK, side='right'),
        N_EXPERTS - 1)
    x_pad = jnp.concatenate([xf, jnp.zeros((1, d), xf.dtype)], axis=0)
    xs = x_pad[slot_tok].reshape(n_blocks, MOE_BLOCK, d)

    def expert_block(args):
        xb, e = args
        hid = jax.nn.silu(xb @ w_gate[e]) * (xb @ w_up[e])
        return hid @ w_down[e]

    ys = lax.map(expert_block, (xs, blk_expert)).reshape(n_slots, d)
    out = jnp.zeros((n + 1, d), ys.dtype).at[slot_tok].add(ys * slot_w[:, None].astype(ys.dtype))
    return out[:n].reshape(shp)

def trunk_layer(x, ctx, c, c_ctx, w_mod, b_mod, norm1_g, w_in, conv_w, a_log, dt_bias, onorm_g, w_out,
                norm2_g, w_group, b_group, w_router, b_router, w_gate, w_up, w_down, update_ctx):
    mod_x = jnp.split((jax.nn.silu(c) @ w_mod + b_mod)[:, None, :], 6, axis=-1)
    mod_c = jnp.split((jax.nn.silu(c_ctx) @ w_mod + b_mod)[None, None, :], 6, axis=-1)

    hc = modulate(rmsnorm_2(ctx, norm1_g), mod_c[0], mod_c[1])
    fc, qc, kc, vc, zc, gc, bc = mixer_features(hc, w_in, conv_w, a_log, dt_bias, conv_seq)
    zero_state = jnp.zeros((ctx.shape[0], DN_HEADS, DK, DV), jnp.float32)
    oc, s_fwd, s_bwd = bidir_delta(qc, kc, vc, gc, bc, zero_state, zero_state)

    hx = modulate(rmsnorm_2(x, norm1_g), mod_x[0], mod_x[1])
    fx, qx, kx, vx, zx, gx, bx = mixer_features(hx, w_in, conv_w, a_log, dt_bias, conv_grid)
    ox, _, _ = bidir_delta(qx, kx, vx, gx, bx, s_fwd, s_bwd)
    x = x + mod_x[2] * mixer_output(fx, ox, zx, onorm_g, w_out)
    x = x + mod_x[5] * moe_ffn(modulate(rmsnorm_2(x, norm2_g), mod_x[3], mod_x[4]),
                               w_group, b_group, w_router, b_router, w_gate, w_up, w_down)
    if update_ctx:
        ctx = ctx + mod_c[2] * mixer_output(fc, oc, zc, onorm_g, w_out)
        ctx = ctx + mod_c[5] * moe_ffn(modulate(rmsnorm_2(ctx, norm2_g), mod_c[3], mod_c[4]),
                                       w_group, b_group, w_router, b_router, w_gate, w_up, w_down)
    return x, ctx

def second_inputs(seed: int = 0) -> dict:
    key = jax.random.key(seed)
    ks = jax.random.split(key, 24)
    nrm = lambda k, shape, s: jax.random.normal(k, shape, jnp.float32) * s
    x = nrm(ks[0], (BATCH, SEQ, D_MODEL), 1.0)
    c = nrm(ks[1], (BATCH, D_MODEL), 1.0)
    ctx = nrm(ks[2], (BATCH, CTX_LEN, D_MODEL), 1.0)
    c_ctx = nrm(ks[3], (D_MODEL,), 1.0)
    w_mod = nrm(ks[4], (DEPTH, D_MODEL, 6 * D_MODEL), 0.5 * D_MODEL ** -0.5)
    b_mod = nrm(ks[5], (DEPTH, 6 * D_MODEL), 0.01)
    norm1_g = 1.0 + nrm(ks[6], (DEPTH, D_MODEL), 0.02)
    w_in = nrm(ks[7], (DEPTH, D_MODEL, W_IN), D_MODEL ** -0.5)
    conv_w = nrm(ks[8], (DEPTH, CONV_K, CONV_K, CONV_CH), 1.0 / CONV_K)
    a_log = jnp.log(jax.random.uniform(ks[9], (DEPTH, 2, DN_HEADS), jnp.float32, 1.0, 16.0))
    dt = jnp.exp(jax.random.uniform(ks[10], (DEPTH, 2, DN_HEADS), jnp.float32,
                                    math.log(1e-3), math.log(1e-1)))
    dt_bias = dt + jnp.log(-jnp.expm1(-dt))
    onorm_g = 1.0 + nrm(ks[11], (DEPTH, DV), 0.02)
    w_out = nrm(ks[12], (DEPTH, MIX_W, D_MODEL), MIX_W ** -0.5)
    norm2_g = 1.0 + nrm(ks[13], (DEPTH, D_MODEL), 0.02)
    w_group = nrm(ks[14], (DEPTH, D_MODEL, N_GROUPS), D_MODEL ** -0.5)
    b_group = nrm(ks[15], (DEPTH, N_GROUPS), 0.01)
    w_router = nrm(ks[16], (DEPTH, D_MODEL, N_EXPERTS), D_MODEL ** -0.5)
    b_router = nrm(ks[17], (DEPTH, N_EXPERTS), 0.01)
    w_gate = nrm(ks[18], (DEPTH, N_EXPERTS, D_MODEL, D_EXPERT), D_MODEL ** -0.5)
    w_up = nrm(ks[19], (DEPTH, N_EXPERTS, D_MODEL, D_EXPERT), D_MODEL ** -0.5)
    w_down = nrm(ks[20], (DEPTH, N_EXPERTS, D_EXPERT, D_MODEL), D_EXPERT ** -0.5)
    final_g = 1.0 + nrm(ks[21], (D_MODEL,), 0.02)
    return {"x": x, "c": c, "ctx": ctx, "c_ctx": c_ctx, "w_mod": w_mod, "b_mod": b_mod,
            "norm1_g": norm1_g, "w_in": w_in, "conv_w": conv_w, "a_log": a_log, "dt_bias": dt_bias,
            "onorm_g": onorm_g, "w_out": w_out, "norm2_g": norm2_g, "w_group": w_group,
            "b_group": b_group, "w_router": w_router, "b_router": b_router, "w_gate": w_gate,
            "w_up": w_up, "w_down": w_down, "final_g": final_g}

def second_block(x, c, ctx, c_ctx, w_mod, b_mod, norm1_g, w_in, conv_w, a_log, dt_bias, onorm_g, w_out,
              norm2_g, w_group, b_group, w_router, b_router, w_gate, w_up, w_down, final_g):
    for l in range(DEPTH):
        x, ctx = trunk_layer(x, ctx, c, c_ctx, w_mod[l], b_mod[l], norm1_g[l], w_in[l], conv_w[l], a_log[l],
                             dt_bias[l], onorm_g[l], w_out[l], norm2_g[l], w_group[l], b_group[l],
                             w_router[l], b_router[l], w_gate[l], w_up[l], w_down[l],
                             update_ctx=(l < DEPTH - 1))
    return rmsnorm_2(x, final_g)


def setup_inputs(seed=0):
    out = dict(first_inputs(seed))
    for name, value in second_inputs(seed + 1).items():
        if name != "x":
            out[name + "_2"] = value
    return out


def reference(
    x, norm_mix_g, w_in, b_in, lam_re, lam_im, log_dt, ssm_b_re, ssm_b_im, ssm_c_re, ssm_c_im,
    ssm_d, w_glu_a, w_glu_b, conv_w, conv_b, w_conv_out, w_out, norm_mlp_g, w_ff1, w_ff2,
    norm_final_g, c_2, ctx_2, c_ctx_2, w_mod_2, b_mod_2, norm1_g_2, w_in_2, conv_w_2, a_log_2,
    dt_bias_2, onorm_g_2, w_out_2, norm2_g_2, w_group_2, b_group_2, w_router_2, b_router_2,
    w_gate_2, w_up_2, w_down_2, final_g_2,
):
    x = first_block(
        x, norm_mix_g, w_in, b_in, lam_re, lam_im, log_dt, ssm_b_re, ssm_b_im, ssm_c_re,
        ssm_c_im, ssm_d, w_glu_a, w_glu_b, conv_w, conv_b, w_conv_out, w_out, norm_mlp_g, w_ff1,
        w_ff2, norm_final_g,
    )
    return second_block(
        x, c_2, ctx_2, c_ctx_2, w_mod_2, b_mod_2, norm1_g_2, w_in_2, conv_w_2, a_log_2,
        dt_bias_2, onorm_g_2, w_out_2, norm2_g_2, w_group_2, b_group_2, w_router_2, b_router_2,
        w_gate_2, w_up_2, w_down_2, final_g_2,
    )


_drawn_inputs = setup_inputs


def setup_inputs(seed=0):
    import zlib

    import numpy as np

    out = dict(_drawn_inputs(seed))
    spreads = {}
    factors = {'lam_re': 64.0,
     'lam_im': 30.208,
     'log_dt': 28.752,
     'ssm_b_re': 39.779,
     'ssm_b_im': 31.544,
     'ssm_c_re': 38.712,
     'ssm_c_im': 40.552,
     'conv_b': 4.546,
     'norm_mlp_g': 2.725,
     'ctx_2': 5.347,
     'c_ctx_2': 8.0,
     'b_mod_2': 4.131,
     'norm1_g_2': 7.313,
     'onorm_g_2': 8.0,
     'norm2_g_2': 4.418,
     'b_group_2': 8.0,
     'b_router_2': 25.938,
     'final_g_2': 8.456}
    for name, (base, spread) in spreads.items():
        noise = np.random.default_rng([zlib.crc32(name.encode()), seed]).standard_normal(out[name].shape)
        drawn = base * np.exp(spread * noise) if base else spread * noise
        out[name] = __import__('jax').numpy.asarray(drawn.astype(out[name].dtype))
    for name, factor in factors.items():
        out[name] = (out[name] * factor).astype(out[name].dtype)
    return out
```

```python
from contextlib import ExitStack

import concourse.bass as bass
import numpy as np
from concourse import mybir

F32 = mybir.dt.float32
I32 = mybir.dt.int32
ALU = mybir.AluOpType
ACT = mybir.ActivationFunctionType
AXX = mybir.AxisListType.X

P = 128
D = 1024
T = 512
TC = 256
KD = D // P
KT = T // P
EPS = 1e-6
SW = 512
NS = 64
SG = 16
NJ = 16
F_FF = 4096
H = 4
NE = 32
FE = 512
CAP = 64
NOV = 15
RSLOTS = 4
UNIT = 4096
MAGIC = 12582912.0
TWO_PI = 6.2831850051879883

CO = {}
_n = 0
for _name, _w in (("ident", P), ("ones", P), ("up", P), ("lo", P), ("up_s", P), ("lo_s", P), ("bd16", P),
                  ("lv16", P), ("lv32", P), ("lv64", P), ("dft", 2 * P), ("t_low", 32), ("t_high", 16),
                  ("e64", 32), ("eidx", 32), ("gidx", 4), ("blk", 16), ("tok", KT)):
    CO[_name] = (_n, _w)
    _n += _w
CW = _n


def constants():
    i = np.arange(P)
    r, c = i[:, None], i[None, :]
    same = lambda s: (r // s == c // s).astype(np.float64)
    ang = 2 * np.pi * (r * c % P) / P
    full = lambda v: np.broadcast_to(np.asarray(v, np.float64), (P, len(v)))
    parts = {
        "ident": np.eye(P), "ones": np.ones((P, P)), "up": r <= c, "lo": r >= c, "up_s": r < c, "lo_s": r > c,
        "bd16": same(16), "lv16": same(32) - same(16), "lv32": same(64) - same(32), "lv64": 1 - same(64),
        "dft": np.concatenate([np.cos(ang), -np.sin(ang)], 1) / np.sqrt(T * P),
        "t_low": full(np.arange(32)), "t_high": full(np.arange(16)), "e64": full(CAP * np.arange(NE)),
        "eidx": full(np.arange(NE)), "gidx": full(np.arange(4)), "blk": full(np.arange(16)),
        "tok": np.arange(KT)[None, :] * P + i[:, None],
    }
    t = np.arange(T)
    angt = 2 * np.pi * (t[:, None] * t[None, :] % T) / T
    return (np.concatenate([np.asarray(parts[n], np.float32) for n in CO], 1),
            np.concatenate([np.cos(angt), np.sin(angt)], 1).astype(np.float32))


def dense_plan():
    units = []

    def unit(name, groups):
        units.append((name, groups))

    unit("-n1", "A" * 8)
    unit("u", "AAAA")
    for h in range(2):
        unit(f"cg{h}", "AAAA")
        unit(f"cv{h}", "DDDD")
        unit(f"bg{h}", "DDDD")
    unit("gc0", "AAAA")
    unit("gc1", "AAAA")
    unit("co0", "DDDD")
    unit("co1", "DDDD")
    unit("gs0", "AAAA")
    unit("gs1", "AAAA")
    unit("ga", "")
    unit("gb", "DA" * 8)
    unit("wo0", "DDDD")
    unit("wo1", "DDDD")
    unit("-n2", "A" * 8)
    m = 0
    for h in range(2):
        for q in range(4):
            unit(f"f1_{h}{q}", "AAAA")
            unit(f"mod{m}", "")
            m += 1
        for q in range(4):
            unit(f"f2_{h}{q}", "DDDD")
            if m < 12:
                unit(f"mod{m}", "")
                m += 1
            if (h, q) == (1, 2):
                unit("-mc", "D")
                unit("-mb", "D" * 8)
    unit("-n3", "A" * 16)
    unit("-gt", "AAD")
    unit("ik", "A" * 8)
    unit("iv", "A" * 8)
    unit("iq", "AAAA")
    unit("iz", "DDDD")
    unit("if", "AAAA")
    unit("-ss", "A" * 12)
    unit("-fa", "A" * 8)
    unit("dft", "AAAA")
    unit("-tk", "AD" * 6)
    unit("-ot", "DDDD")
    unit("wp0", "DDDD")
    unit("wp1", "DDDD")
    unit("-n5", "A" * 8)
    unit("-lg", "AD")
    unit("-cn", "D")
    return units


class Count:

    def __init__(self, sem):
        self.sem, self.n = sem, 0

    def done(self, eng, ins):
        self.n += 1
        ins.then_inc(self.sem, 1)
        eng.wait_ge(self.sem, self.n)


def program(nc, a, out):
    units = dense_plan()
    names = [u for u, _ in units if u[0] != "-"]
    first_group, total = {}, 0
    groups = []
    seen = {"A": 0, "D": 0}
    for name, ev in units:
        first_group[name] = total
        for e in ev:
            groups.append((e, seen[e]))
            seen[e] += 1
            total += 1
    last_group = {n: first_group[n] + len(ev) for n, ev in units}
    last_group["ga"] = last_group["gb"]

    with ExitStack() as ctx:
        def sb(name, shape, dt=F32):
            return ctx.enter_context(nc.sbuf_tensor(name, shape, dt))

        sems = {}

        def sem(name):
            if name not in sems:
                sems[name] = ctx.enter_context(nc.semaphore(name))
            return sems[name]

        K1 = 256
        arena = sb("arena", [P, 193 * K1])

        def at(kib, kib_n):
            return arena[:, int(kib * K1):int((kib + kib_n) * K1)]

        ring = [at(16 * s, 16) for s in range(RSLOTS)]
        res = at(64, 16).rearrange("p (k d) -> p k d", k=KT)
        xT = at(80, 16).rearrange("p (c t) -> p c t", c=KD)
        U = at(96, 8).rearrange("p (c t) -> p c t", c=4)
        VT = at(104, 8).rearrange("p (c t) -> p c t", c=4)
        CT = at(112, 8).rearrange("p (c t) -> p c t", c=4)
        YB = at(120, 16).rearrange("p (c t) -> p c t", c=KD)
        GC = at(136, 16).rearrange("p (c t) -> p c t", c=KD)
        xn = at(120, 16).rearrange("p (k d) -> p k d", k=KT)
        H1 = at(104, 32).rearrange("p (c t) -> p c t", c=16)
        modacc = at(136, 32)
        xn2 = at(168, 16).rearrange("p (k d) -> p k d", k=KT)
        bbT = at(152, 4).rearrange("p (q r s) -> p q r s", q=4, r=2)
        cbd = at(156, 4).rearrange("p (r j g c) -> p r j g c", r=2, j=NJ, g=2)
        bbd = at(160, 4).rearrange("p (r j g c) -> p r j g c", r=2, j=NJ, g=2)
        bld = at(164, 2).rearrange("p (r j c) -> p r j c", r=2, j=NJ)
        cld = at(166, 4).rearrange("p (r q d n) -> p r q d n", r=2, q=4, d=2)
        gelu_b = at(160, 6).rearrange("p (b t) -> p b t", b=3)
        rot_t = at(166, 4).rearrange("p (b t) -> p b t", b=2)
        ssm_w = at(64, 16).rearrange("p (b t) -> p b t", b=8)
        rot = at(170, 8).rearrange("p (b r t) -> p b r t", b=2, r=2)
        tab_h = at(178, 2).rearrange("p (r j n) -> p r j n", r=2, j=NJ)
        tab_l = at(180, 4).rearrange("p (r j n) -> p r j n", r=2, j=NJ)

        n2g = at(96, 4)
        modb = at(168, 16)
        ctr = at(120, 8).rearrange("p (k d) -> p k d", k=2)
        xn3 = at(104, 16).rearrange("p (k d) -> p k d", k=KT)
        hcT = at(96, 8).rearrange("p (c t) -> p c t", c=KD)
        fT = at(104, 8).rearrange("p (c t) -> p c t", c=4)
        gT = at(104, 3)
        mixF = at(112, 8).rearrange("p (c t) -> p c t", c=4)
        mixO = at(104, 8).rearrange("p (c t) -> p c t", c=4)
        oacc = at(120, 8).rearrange("p (k h d) -> p k h d", k=KT, h=H)
        qT = at(128, 8).rearrange("p (h t) -> p h t", h=H)
        kT = at(136, 8).rearrange("p (h t) -> p h t", h=H)
        vT = at(144, 8).rearrange("p (h t) -> p h t", h=H)
        zT = at(152, 8).rearrange("p (h t) -> p h t", h=H)
        kcT = at(160, 4).rearrange("p (h t) -> p h t", h=H)
        vcT = at(164, 4).rearrange("p (h t) -> p h t", h=H)
        cbuf = at(112, 4).rearrange("p (b t) -> p b t", b=2)
        tbuf = at(116, 4).rearrange("p (b t) -> p b t", b=2)
        sqb = at(120, 4).rearrange("p (b t) -> p b t", b=2)
        rtb = at(124, 4).rearrange("p (b t) -> p b t", b=2)
        raw = at(184, 6)[:, 0:1320].rearrange("p (b y x) -> p b y x", b=2, y=10)
        rawc = at(190, 3)[:, 0:516].rearrange("p (b x) -> p b x", b=2)
        fy = at(80, 16).rearrange("p (k q n) -> p k q n", k=KT, q=4)
        ktok = at(80, 12).rearrange("p (c h d) -> p c h d", c=6, h=H)
        vtok = at(92, 12).rearrange("p (c h d) -> p c h d", c=6, h=H)
        WS = [at(16 + 2 * i, 2) for i in range(8)] + [at(144 + 2 * i, 2) for i in range(4)] + [at(184, 2), at(186, 2)]
        V4 = lambda x: x.rearrange("p (h i) -> p h i", h=H)
        S = at(164, 4).rearrange("p (d h e) -> p d h e", d=2, h=H)

        xm = at(128, 16).rearrange("p (k d) -> p k d", k=KT)
        GU = [at(b, 32).rearrange("p (g k n) -> p g k n", g=2, k=KD) for b in (16, 80)]
        WD = [at(b, 16).rearrange("p (k n) -> p k n", k=4) for b in (48, 112)]
        XE = [at(154 + 2 * s, 2) for s in range(2)]
        XG = [at(158 + 2 * s, 2).rearrange("p (c n) -> p c n", c=4) for s in range(2)]
        TB = [at(162 + s, 1) for s in range(2)]
        SB = [at(164 + s, 1) for s in range(2)]
        HB = [at(166 + s, 1) for s in range(2)]
        HT = [at(190 + s, 1).rearrange("p (c n) -> p c n", c=2) for s in range(2)]
        YO = [at(144 + 2 * s, 2) for s in range(2)]
        lgT = at(152, 2)
        rt = lambda n, w=NE: at(144, 8)[:, P * n:P * n + KT * w].rearrange("p (k e) -> p k e", k=KT)
        fgb = at(184, 4)
        wr = at(188, 2)[:, 0:KD * 36].rearrange("p (k n) -> p k n", k=KD)
        rb = at(192, 1)[:, 0:36]
        YG = at(0, 32).rearrange("p (a k d) -> p a k d", a=2, k=KT)
        xs = nc.dram_tensor("expert_in", [CAP * (NE + NOV + 1), D], F32, kind="Internal").ap()
        ys = nc.dram_tensor("expert_out", [CAP * (NE + NOV + 1), D], F32, kind="Internal").ap()
        zero = at(188, 4)

        cst = sb("cst", [P, CW])
        C = {n: cst[:, o:o + w] for n, (o, w) in CO.items()}
        ident, ones = C["ident"], C["ones"]
        rows = sb("rows", [P, 3, P])
        c1 = sb("c1", [P, 3, P])
        ldt = sb("ldt", [NJ, 2])
        ldtr = sb("ldtr", [NJ, P])
        sm = sb("sm", [P, 40, NJ])
        smi = sb("smi", [P, NJ], I32)
        sc = sb("sc", [P, 2, 16])
        st = sb("st", [P, 8, 8])
        mc = sb("mc", [P, 4, 8])
        wg = sb("wg", [P, KD * 16])[:].rearrange("p (k n) -> p k n", k=KD)
        gkb = sb("gkb", [P, 2, 8])
        eps4 = sb("eps4", [P, 1])
        tk = sb("tk", [P, 24, KT])
        idx = sb("idx", [P, 2, KT], I32)
        pad = sb("pad", [P, 1])
        ovi = sb("ovi", [P, 17], I32)
        gk = sm[:].rearrange("p a b -> p (a b)")[:, 0:13 * 48].rearrange("p (k d c h) -> p k d c h", k=13, d=2, c=6)
        bhalf = sb("bhalf", [P, 44])
        gfb = at(184, 4)

        PB = [ctx.enter_context(nc.psum_tensor(f"pb{n}", [P, 512], F32)) for n in range(8)]

        col = lambda t, n: c1[:, t, n:n + 1]
        b_in_col = lambda n: col(0, n)
        conv_w_col = lambda k, c: col(0, 44 + 8 * k + c)
        conv_b_col = lambda c: col(0, 68 + c)

        block = ctx.enter_context(nc.Block())

        def unit_view(name):
            slot = ring[names.index(name) % RSLOTS]
            cols = lambda w, c0, n=512: w[:, c0:c0 + n].rearrange("(k p) n -> p k n", p=P)
            k8 = slot.rearrange("p (k n) -> p k n", k=8)
            k4 = slot.rearrange("p (k n) -> p k n", k=4)
            k16 = slot.rearrange("p (k n) -> p k n", k=16)
            h = int(name[-1]) if name[-1].isdigit() else 0
            w_in = a["w_in"][0]
            if name == "u":
                return k8, cols(w_in, 0)
            for key, c0 in (("bg", 512), ("cg", 1536), ("cv", 2560), ("gs", 3584), ("gc", 4608)):
                if name[:2] == key:
                    return k8, cols(w_in, c0 + 512 * h)
            if name[:2] == "co":
                return k8, cols(a["w_conv_out"][0], 512 * h)
            if name[:2] == "wo":
                return k8, cols(a["w_out"][0], 512 * h)
            if name in ("ga", "gb"):
                return k4, a["w_glu_" + name[1]][0].rearrange("(k p) n -> p k n", p=P)
            if name[:2] == "f1":
                return k8, cols(a["w_ff1"][0], 2048 * int(name[3]) + 512 * int(name[4]))
            if name[:2] == "f2":
                return k16, a["w_ff2"][0][2048 * int(name[3]):2048 * int(name[3]) + 2048,
                                          256 * int(name[4]):256 * int(name[4]) + 256].rearrange(
                                              "(k p) n -> p k n", p=P)
            if name in ("ik", "iv", "iq", "iz", "if"):
                return k8, cols(a["w_in_2"][0], {"f": 0, "q": 512, "k": 1024, "v": 1536, "z": 2048}[name[1]])
            if name == "dft":
                return k4, a["dft_t"].rearrange("(k p) n -> p k n", p=P)
            if name[:2] == "wp":
                return k8, cols(a["w_out_2"][0], 512 * h)
            if name[:3] == "mod":
                return k8, cols(a["w_mod_2"][0], 512 * int(name[3:]))
            raise KeyError(name)

        W = {n: unit_view(n)[0] for n in names}
        mod_units = [n for n in names if n[:3] == "mod"]

        def loaded(eng, name):
            n = names.index(name)
            eng.wait_ge(sem(f"unit_loaded{n % RSLOTS}"), 16 * (n // RSLOTS + 1))

        def freed(eng, name):
            if name in mod_units:
                eng.wait_ge(sem("mod_unit_used"), mod_units.index(name) + 1)
            else:
                eng.wait_ge(sem("group_done"), last_group[name])

        def evacuated(eng, g):
            e, n = groups[g]
            eng.wait_ge(sem({"A": "act_evac", "D": "dve_evac"}[e]), n + 1)

        def unit_evacuated(eng, name):
            evacuated(eng, last_group[name] - 1)

        def act_loads(act):
            row_loads = []
            for t, lo, n, src in ((0, 0, 44, a["b_in"][0]), (0, 68, 8, a["conv_b"][0]), (0, 76, 8, a["norm_mix_g"][0]),
                                  (0, 84, 4, a["ssm_d"][0]), (1, 0, 8, a["norm_mlp_g"][0]),
                                  (1, 116, 8, a["norm1_g_2"][0]), (1, 124, 1, a["onorm_g_2"][0]),
                                  (2, 0, 8, a["c_2"][0]), (2, 8, 8, a["c_ctx_2"]), (2, 16, 16, a["b_mod_2"][0, 0:2048])):
                row_loads.append((rows[lo:lo + n, t, :], src.rearrange("(r p) -> r p", p=P)))
            row_loads.append((rows[44:68, 0, :], a["conv_w"][0].rearrange("k (r p) -> (k r) p", p=P)))
            row_loads.append((rows[88:104, 0, :], a["lam_re"][0].rearrange("(j g) n -> j (g n)", g=2)))
            row_loads.append((rows[104:120, 0, :], a["lam_im"][0].rearrange("(j g) n -> j (g n)", g=2)))
            row_loads.append((rows[8:116, 1, :], a["conv_w_2"][0].rearrange("y x (r p) -> (y x r) p", p=P)))
            row_loads.append((ldt[:], a["log_dt"][0].rearrange("(j g) -> j g", g=2)))
            for dst, src in row_loads:
                act.dma_start(dst, src).then_inc(sem("rows_loaded"), 16)
            for r, w in enumerate(("ssm_b_re", "ssm_b_im")):
                act.dma_start(bld[:, r], a[w][0].rearrange("(j g) n c -> (g n) j c", g=2)).then_inc(sem("b_loaded"), 16)
            for r, w in enumerate(("ssm_c_re", "ssm_c_im")):
                for d in range(2):
                    act.dma_start(cld[:, r, :, d], a[w][0].rearrange("(q g) c n -> (g c) q n", q=4)).then_inc(
                        sem("c_loaded"), 16)
            return len(row_loads)

        N_ROWS = 15

        def act_squares(act, src, nk, junk, tag):
            for k in range(nk):
                nc.scalar.activation(junk, src[:, k], ACT.Square, accum_out=st[:, 0, k:k + 1]).then_inc(
                    sem("squares_" + tag), 1)
                act.wait_ge(sem("squares_" + tag), k + 1)

        def dve_rstd(dve, chain, nk, width, tag, row=0):
            dve.wait_ge(sem("squares_" + tag), nk)
            chain.done(dve, nc.vector.tensor_scalar(st[:, 1, 0:nk], st[:, 0, 0:nk], 1.0 / width, EPS, ALU.mult, ALU.add))
            nc.vector.tensor_copy(st[:, 2, 0:nk], st[:, 1, 0:nk]).then_inc(sem("mean_" + tag), 1)
            dve.wait_ge(sem("root_" + tag), 1)
            chain.done(dve, nc.vector.reciprocal(st[:, 4, 0:nk], st[:, 3, 0:nk]))

        def act_root(act, nk, tag):
            act.wait_ge(sem("mean_" + tag), 1)
            nc.scalar.activation(st[:, 3, 0:nk], st[:, 2, 0:nk], ACT.Sqrt).then_inc(sem("root_" + tag), 1)

        def dve_scale_rows(dve, src, dst, nk, tag):
            for k in range(nk):
                nc.vector.tensor_scalar(dst[:, k], src[:, k], st[:, 4, k:k + 1], None, ALU.mult).then_inc(
                    sem("rows_" + tag), 1)

        def pe_turn(pe, src, nk, tag, first=0):
            for c in range(KD):
                g = first_group["-" + tag] + first + c
                if g >= 4:
                    evacuated(pe, g - 4)
                for k in range(nk):
                    l = nc.tensor.transpose(PB[g % 4][:, k * P:(k + 1) * P], src[:, k, c * P:(c + 1) * P], ident)
                l.then_inc(sem("group_done"), 1)

        def act_turned(act, dst, nk, tag, scale, bias=None, first=0):
            for c in range(KD):
                g = first_group["-" + tag] + first + c
                act.wait_ge(sem("group_done"), g + 1)
                nc.scalar.activation(dst[:, c, 0:nk * P], PB[g % 4][:, 0:nk * P], ACT.Identity, scale=scale(c),
                                     bias=bias(c) if bias else 0.0).then_inc(sem("act_evac"), 1)

        def pe_group(pe, g, o, lhs, rhs):
            if g >= 4:
                evacuated(pe, g - 4)
            n = len(lhs)
            for i in range(n):
                l = nc.tensor.matmul(o, lhs[i], rhs[i], start=(i == 0), stop=(i == n - 1))
            l.then_inc(sem("group_done"), 1)

        def pe_unit_T(pe, name, src, kn, cols=range(4), width=T):
            g0 = first_group[name]
            for i, m in enumerate(cols):
                pe_group(pe, g0 + i, PB[(g0 + i) % 4][:, 0:width], [W[name][:, k, m * P:(m + 1) * P] for k in range(kn)],
                         [src[:, k, 0:width] for k in range(kn)])

        def pe_unit_R(pe, name, src, kn, width=512):
            g0 = first_group[name]
            for k in range(KT):
                pe_group(pe, g0 + k, PB[(g0 + k) % 4][:, 0:width], [src[:, c, k * P:(k + 1) * P] for c in range(kn)],
                         [W[name][:, c, 0:width] for c in range(kn)])

        BETA, G, GCUM, EG, NEG, KDEC, ETOT = range(7)
        batches = [b for i in range(6) for b in ((0, (4, 5, 0, 1, 2, 3)[i]), (1, (5, 4, 3, 2, 1, 0)[i]))]
        conv_jobs = ([("ik", i, kT, 4) for i in range(4)] + [("ik", 4 + i, kcT, 4) for i in range(4)]
                     + [("iv", i, vT, 8) for i in range(4)] + [("iv", 4 + i, vcT, 8) for i in range(4)]
                     + [("iq", i, qT, 0) for i in range(4)])
        norm_jobs = [(kT, i, 1.0, T) for i in range(4)] + [(kcT, i, 1.0, TC) for i in range(4)] + [
            (qT, i, P ** -0.5, T) for i in range(4)]

        def pe_mod(pe):
            pe.wait_ge(sem("mod_unit_used"), 12)
            g = first_group["-mc"]
            evacuated(pe, g - 4)
            for i in range(32):
                o = 128 * i if i < 16 else 6144 + 128 * (i - 16)
                l = nc.tensor.matmul(PB[g % 4][:, i:i + 1], modacc[:, o:o + P], ones[:, 0:1], start=True, stop=True)
            l.then_inc(sem("group_done"), 1)
            g = first_group["-mb"]
            for i in range(8):
                pe_group(pe, g + i, PB[(g + i) % 4][:], [ones], [modacc[:, 2048 + 512 * i:2560 + 512 * i]])

        def dve_mod(dve, ch, do, bank):
            STT, TT = nc.vector.scalar_tensor_tensor, nc.vector.tensor_tensor
            g = first_group["-mc"]
            ps = bank(g)
            mcf = mc[:].rearrange("p a b -> p (a b)")
            for i in range(2):
                ins = TT(mcf[:, 16 * i:16 * i + 16], ps[:, 16 * i:16 * i + 16], c1[:, 2, 16:32], ALU.add)
                if i:
                    ins.then_inc(sem("dve_evac"), 1)
                    evacuated(dve, g)
                else:
                    do(ins)
            for i in (1, 3):
                STT(mc[:, i], mc[:, i], 1.0, c1[:, 1, 116:124], ALU.add, ALU.mult).then_inc(sem("mc_ready"), 1)
            g = first_group["-mb"]
            dve.wait_ge(sem("bmod_loaded"), 32)
            for i in range(8):
                ps = bank(g + i)
                v = modb[:, 512 * i:512 * i + 512]
                TT(v, ps[:], v, ALU.add).then_inc(sem("dve_evac"), 1)
            evacuated(dve, g + 7)
            do(STT(modb[:, 2048:3072], modb[:, 2048:3072], 1.0, n2g, ALU.add, ALU.mult))

        def pe_second(pe):
            pe.wait_ge(sem("rows_n3"), KT)
            pe_turn(pe, xn3, KT, "n3")
            pe.wait_ge(sem("rows_nc"), 2)
            pe_turn(pe, ctr, 2, "n3", 8)
            unit_evacuated(pe, "-n3")
            g = first_group["-gt"]
            pe.wait_ge(sem("wg_loaded"), 48)
            pe_group(pe, g, PB[g % 4][0:16, :], [wg[:, k] for k in range(KD)], [xT[:, k] for k in range(KD)])
            pe_group(pe, g + 1, PB[(g + 1) % 4][0:16, 0:TC], [wg[:, k] for k in range(KD)], [hcT[:, k] for k in range(KD)])
            evacuated(pe, g + 1)
            evacuated(pe, g - 2)
            for c in range(6):
                l = nc.tensor.transpose(PB[(g + 2) % 4][:, 16 * c:16 * c + 16], gT[0:16, c * P:c * P + P], ident[0:16, 0:16])
            l.then_inc(sem("group_done"), 1)
            for name in ("ik", "iv", "iq", "iz", "if"):
                loaded(pe, name)
                g0 = first_group[name]
                for i in range(last_group[name] - g0):
                    src, w = (xT, T) if i < 4 else (hcT, TC)
                    m = i % 4
                    pe_group(pe, g0 + i, PB[(g0 + i) % 4][:, 0:w], [W[name][:, k, m * P:(m + 1) * P] for k in range(KD)],
                             [src[:, k, 0:w] for k in range(KD)])
                if name == "iq":
                    pe.wait_ge(sem("g_ready"), 1)
                    for d in range(2):
                        nc.tensor.matmul(PB[4][:, 24 * d:24 * d + 24], C[("up", "lo")[d]],
                                         gk[:, G, d].rearrange("p c h -> p (c h)"), start=True, stop=True)
                    nc.tensor.matmul(PB[4][:, 48:96], ones, gk[:, G].rearrange("p d c h -> p (d c h)"), start=True,
                                     stop=True).then_inc(sem("g_sums"), 1)
            g0 = first_group["-ss"]
            for m, (t, i, s, w) in enumerate(norm_jobs):
                pe.wait_ge(sem("sq_ready"), m + 1)
                pe_group(pe, g0 + m, PB[(g0 + m) % 4][:, 0:w], [ones], [sqb[:, m % 2, 0:w]])
            unit_evacuated(pe, "if")
            g0 = first_group["-fa"]
            for k in range(KT):
                for q in range(2):
                    g = g0 + 2 * k + q
                    evacuated(pe, g - 4)
                    for i in range(2):
                        l = nc.tensor.matmul(PB[g % 4][:, 256 * i:256 * i + 256], fT[:, 2 * q + i, k * P:(k + 1) * P],
                                             C["dft"], start=True, stop=True)
                    l.then_inc(sem("group_done"), 1)
            unit_evacuated(pe, "-fa")
            loaded(pe, "dft")
            g0 = first_group["dft"]
            for q in range(4):
                pe_group(pe, g0 + q, PB[(g0 + q) % 4][:],
                         [fy[:, k, q, P * r:P * r + P] for k in range(KT) for r in range(2)],
                         [W["dft"][:, k, T * r:T * r + T] for k in range(KT) for r in range(2)])
            pe.wait_ge(sem("qkv_ready"), 20)
            pe.wait_ge(sem("normed"), 12)
            g0 = first_group["-tk"]
            for c in range(6):
                for i, (x, xc) in enumerate(((kT, kcT), (vT, vcT))):
                    g = g0 + 2 * c + i
                    evacuated(pe, g - 4)
                    for h in range(H):
                        src = x[:, h, c * P:(c + 1) * P] if c < 4 else xc[:, h, (c - 4) * P:(c - 3) * P]
                        l = nc.tensor.transpose(PB[g % 4][:, h * P:(h + 1) * P], src, ident)
                    l.then_inc(sem("group_done"), 1)
            unit_evacuated(pe, "-tk")
            evacuated(pe, last_group["-tk"] - 2)
            for n in range(12):
                pe_delta(pe, n)
            pe.wait_ge(sem("o_ready"), 1)
            g0 = first_group["-ot"]
            for h in range(H):
                for k in range(KT):
                    l = nc.tensor.transpose(PB[(g0 + h) % 4][:, k * P:(k + 1) * P], oacc[:, k, h], ident)
                l.then_inc(sem("group_done"), 1)
            unit_evacuated(pe, "-ot")
            mix = [mixF[:, c] for c in range(4)] + [mixO[:, c] for c in range(4)]
            for name in ("wp0", "wp1"):
                loaded(pe, name)
                g0 = first_group[name]
                for k in range(KT):
                    pe_group(pe, g0 + k, PB[(g0 + k) % 4][:], [m[:, k * P:(k + 1) * P] for m in mix],
                             [W[name][:, c] for c in range(KD)])
            pe_router(pe)
            pe_experts(pe)

        (GR, E, AT, MU, MS1, _, _, R_, _, _, VN, KD_, MS0, TMP) = WS
        MS = (MS0, MS1)
        NX = at(26, 4).rearrange("p (f u h i) -> p f u h i", f=2, u=2, h=2)
        TX = at(144, 4).rearrange("p (f u h i) -> p f u h i", f=2, u=2, h=2)
        LO, UP = 0, 1
        half = lambda x, f: x[:, f].rearrange("p u h i -> p (u h i)")

        def pe_quad(pe, b, lhs, rhs, name):
            for h in range(H):
                l = nc.tensor.matmul(PB[b][:, h * P:(h + 1) * P], lhs(h), rhs(h), start=True, stop=True)
            l.then_inc(sem(name), 1)

        def pe_delta(pe, n):
            d, c = batches[n]
            lat = c < 4
            m4 = lambda x: (lambda h: V4(x)[:, h])
            kx = (lambda h: kT[:, h, c * P:(c + 1) * P]) if lat else (lambda h: kcT[:, h, (c - 4) * P:(c - 3) * P])
            qx = lambda h: qT[:, h, c * P:(c + 1) * P]
            def pairs(b, f, jobs, name):
                for u, lhs, rhs in jobs:
                    for h in range(2):
                        l = nc.tensor.matmul(PB[b][:, 256 * u + P * h:256 * u + P * h + P], lhs(f, h), rhs(f, h),
                                             start=True, stop=True)
                l.then_inc(sem(name), 1)

            nx = lambda u: (lambda f, h: NX[:, f, u, h])
            tx = lambda u: (lambda f, h: TX[:, f, u, h])
            squares = ((LO, nx(UP), nx(LO)), (UP, nx(LO), nx(UP)))
            if n == 0:
                pe_first_products(pe, 0)
            pe.wait_ge(sem("d_mu"), n + 1)
            for h in range(H):
                l = nc.tensor.transpose(PB[3][:, h * P:(h + 1) * P], V4(MU)[:, h], ident)
            l.then_inc(sem("d_mt"), 1)
            s = lambda h: S[:, d, h]
            if n >= 2:
                pe.wait_ge(sem("d_s"), n - 1)
            pe_quad(pe, 0, kx, s, "d_ks")
            if lat:
                pe_quad(pe, 1, qx, s, "d_qs")
            for f in range(2):
                pe.wait_ge(sem("d_base"), 4 * n + 3 + f)
                pairs(6 + f, f, squares, "d_sq")
            for r in range(3):
                for f in range(2):
                    pe.wait_ge(sem("d_sqc"), 6 * n + 2 * r + f + 1)
                    if r:
                        pe.wait_ge(sem("d_upc"), 12 * n + 2 * r - 1 + f)
                    pairs(4 + f, f, ((LO, nx(UP), tx(LO)), (UP, nx(LO), tx(UP))), "d_up")
                    if r < 2:
                        pairs(6 + f, f, squares, "d_sq")
            for r in range(3):
                pe.wait_ge(sem("d_ms"), 3 * n + r + 1)
                ms = lambda f, h: V4(MS[r % 2])[:, 2 * f + h]
                for f in range(2):
                    pe.wait_ge(sem("d_upc"), 12 * n + 5 + 2 * r + f)
                    pairs(6 + f, f, ((LO, ms, tx(LO)),), "d_pm")
                for f in range(2):
                    pe.wait_ge(sem("d_pmc"), 6 * n + 2 * r + f + 1)
                    pairs(4 + f, f, ((UP, nx(LO), tx(UP)),) + (((LO, tx(UP), nx(LO)),) if r < 2 else ()), "d_up")
            if n + 1 < 12:
                pe.wait_ge(sem("d_state"), n + 1)
                pe_first_products(pe, n + 1)
            pe.wait_ge(sem("d_upc"), 12 * n + 12)
            pe.wait_ge(sem("d_r"), n + 1)
            pe_quad(pe, 2, lambda h: TX[:, h // 2, UP, h % 2], m4(R_), "d_v")
            pe.wait_ge(sem("d_vn"), n + 1)
            pe_quad(pe, 6, m4(KD_), m4(VN), "d_su")
            if lat:
                pe_quad(pe, 3, m4(AT), m4(VN), "d_o")
            if n + 1 < 12:
                pe_row(pe, n + 1)

        def pe_first_products(pe, n):
            d, c = batches[n]
            kx = (lambda h: kT[:, h, c * P:(c + 1) * P]) if c < 4 else (lambda h: kcT[:, h, (c - 4) * P:(c - 3) * P])
            pe_quad(pe, 0, kx, kx, "d_kk")
            if c < 4:
                pe_quad(pe, 1, kx, lambda h: qT[:, h, c * P:(c + 1) * P], "d_kq")
            if n == 0:
                pe_row(pe, 0)

        def pe_row(pe, n):
            pe.wait_ge(sem("d_gr"), n + 1)
            nc.tensor.matmul(PB[2][:], ones, GR, start=True, stop=True).then_inc(sem("d_row"), 1)

        def act_second(act, group):
            act.wait_ge(sem("group_done"), last_group["f2_13"])
            act.dma_start(ctr, a["ctx_2"][0].rearrange("(k p) d -> p k d", p=P)).then_inc(sem("ctx_loaded"), 16)
            for k in range(KT):
                act.wait_ge(sem("x1_ready"), k + 1)
                nc.scalar.activation(at(136, 4), res[:, k], ACT.Square, accum_out=st[:, 5, k:k + 1]).then_inc(
                    sem("squares_n4"), 1)
                act.wait_ge(sem("squares_n4"), k + 1)
            act.wait_ge(sem("ctx_loaded"), 16)
            for k in range(2):
                nc.scalar.activation(at(136, 4), ctr[:, k], ACT.Square, accum_out=st[:, 5, 4 + k:5 + k]).then_inc(
                    sem("squares_n4"), 1)
                act.wait_ge(sem("squares_n4"), KT + k + 1)
            act.wait_ge(sem("mean_n4"), 1)
            nc.scalar.activation(st[:, 7, 0:6], st[:, 6, 0:6], ACT.Sqrt).then_inc(sem("root_n4"), 1)
            act.wait_ge(sem("mc_ready"), 2)
            act_turned(act, xT, KT, "n3", lambda c: mc[:, 1, c:c + 1], lambda c: mc[:, 0, c:c + 1])
            act_turned(act, hcT, 2, "n3", lambda c: mc[:, 3, c:c + 1], lambda c: mc[:, 2, c:c + 1], 8)
            g = first_group["-gt"]
            for i, (o, w) in enumerate(((0, T), (T, TC))):
                act.wait_ge(sem("group_done"), g + i + 1)
                nc.scalar.activation(gT[0:16, o:o + w], PB[(g + i) % 4][0:16, 0:w], ACT.Copy).then_inc(sem("act_evac"), 1)
            act.wait_ge(sem("gate_in"), 1)
            nc.scalar.activation(gk[:, 10], gk[:, 7], ACT.Tanh, scale=0.5).then_inc(sem("gate_out"), 1)
            nc.scalar.activation(gk[:, 11], gk[:, 9], ACT.Exp, scale=-1.0).then_inc(sem("gate_out"), 1)
            nc.scalar.activation(gkb[:, 1], gkb[:, 1], ACT.Exp).then_inc(sem("gate_out"), 1)
            act.wait_ge(sem("raw_zero"), 2)

            def tanh(n):
                name, i, _, _ = conv_jobs[n]
                w = T if i < 4 else TC
                act.wait_ge(sem("taps_done"), n + 1)
                nc.scalar.activation(tbuf[:, n % 2, 0:w], cbuf[:, n % 2, 0:w], ACT.Tanh, scale=0.5).then_inc(
                    sem("taps_tanh"), 1)

            for n, (name, i, _, _) in enumerate(conv_jobs):
                g = first_group[name] + i
                act.wait_ge(sem("group_done"), g + 1)
                if n >= 2:
                    act.wait_ge(sem("taps_done"), n - 1)
                if i < 4:
                    dst, src = raw[:, n % 2, 1:9, 1:65], PB[g % 4][:].rearrange("p (y x) -> p y x", y=8)
                else:
                    dst, src = rawc[:, n % 2, 1:257], PB[g % 4][:, 0:TC]
                nc.scalar.activation(dst, src, ACT.Copy).then_inc(sem("act_evac"), 1)
                if n:
                    tanh(n - 1)
            tanh(len(conv_jobs) - 1)
            act.wait_ge(sem("gdiff"), 1)
            nc.scalar.activation(gk[:, EG], gk[:, GCUM], ACT.Exp).then_inc(sem("gexp"), 1)
            nc.scalar.activation(gk[:, KDEC], gk[:, 12], ACT.Exp).then_inc(sem("gexp"), 1)
            nc.scalar.activation(gk[:, ETOT], gk[:, ETOT], ACT.Exp).then_inc(sem("gexp"), 1)
            for c in range(4):
                g = first_group["iz"] + c
                act.wait_ge(sem("group_done"), g + 1)
                if c >= 2:
                    evacuated(act, g - 2)
                else:
                    act.wait_ge(sem("qkv_ready"), 19 + c)
                nc.scalar.activation(tbuf[:, c % 2], PB[g % 4][:], ACT.Tanh, scale=0.5).then_inc(sem("z_tanh"), 1)
            for c in range(4):
                g = first_group["if"] + c
                act.wait_ge(sem("group_done"), g + 1)
                nc.scalar.activation(fT[:, c], PB[g % 4][:], ACT.Copy).then_inc(sem("act_evac"), 1)
            g0 = first_group["-ss"]
            for m in range(13):
                if m < 12:
                    t, i, s, w = norm_jobs[m]
                    if m >= 2:
                        act.wait_ge(sem("group_done"), g0 + m - 1)
                    nc.scalar.activation(sqb[:, m % 2, 0:w], t[:, i], ACT.Square).then_inc(sem("sq_ready"), 1)
                if m:
                    t, i, s, w = norm_jobs[m - 1]
                    g = g0 + m - 1
                    act.wait_ge(sem("group_done"), g + 1)
                    if m >= 3:
                        act.wait_ge(sem("normed"), m - 2)
                    nc.scalar.activation(rtb[:, (m - 1) % 2, 0:w], PB[g % 4][:, 0:w], ACT.Sqrt, bias=eps4[:]).then_inc(
                        sem("act_evac"), 1)
            for i in range(8):
                g = first_group["-fa"] + i
                act.wait_ge(sem("group_done"), g + 1)
                nc.scalar.activation(fy[:, i // 2, 2 * (i % 2):2 * (i % 2) + 2].rearrange("p q n -> p (q n)"),
                                     PB[g % 4][:], ACT.Copy).then_inc(sem("act_evac"), 1)
            for q in range(4):
                g = first_group["dft"] + q
                act.wait_ge(sem("group_done"), g + 1)
                nc.scalar.activation(mixF[:, q], PB[g % 4][:], ACT.Copy).then_inc(sem("act_evac"), 1)
            for c in range(6):
                g = first_group["-tk"] + 2 * c
                act.wait_ge(sem("group_done"), g + 1)
                nc.scalar.activation(ktok[:, c].rearrange("p h d -> p (h d)"), PB[g % 4][:], ACT.Copy).then_inc(
                    sem("act_evac"), 1)
            for n in range(12):
                act_delta(act, n)
            act.wait_ge(sem("o_sum"), 1)
            act.wait_ge(sem("o_mean"), 1)
            nc.scalar.activation(osq[:, 16:32], osq[:, 0:16], ACT.Sqrt).then_inc(sem("o_root"), 1)
            act_moe(act)

        osq = sm[:].rearrange("p a b -> p (a b)")[:, 0:48]

        def act_delta(act, n):
            act.wait_ge(sem("d_diff"), n + 1)
            nc.scalar.activation(E, E, ACT.Exp).then_inc(sem("d_exp"), 1)
            for r in range(3):
                for f in range(2):
                    act.wait_ge(sem("d_sq"), 6 * n + 2 * r + f + 1)
                    if r:
                        act.wait_ge(sem("d_up"), 12 * n + 2 * r - 1 + f)
                    nc.scalar.activation(half(NX, f), PB[6 + f][:], ACT.Copy).then_inc(sem("d_sqc"), 1)
            for r in range(3):
                for f in range(2):
                    act.wait_ge(sem("d_pm"), 6 * n + 2 * r + f + 1)
                    nc.scalar.activation(NX[:, f, LO].rearrange("p h i -> p (h i)"), PB[6 + f][:, 0:256],
                                         ACT.Copy).then_inc(sem("d_pmc"), 1)

        def dve_second(dve, ch, do, bank):
            V = nc.vector
            TT, TS, STT = V.tensor_tensor, V.tensor_scalar, V.scalar_tensor_tensor
            V.memset(eps4[:], 4 * EPS).then_inc(sem("raw_zero"), 1)
            dve.wait_ge(sem("squares_n4"), 6)
            TS(st[:, 6, 0:6], st[:, 5, 0:6], 1.0 / D, EPS, ALU.mult, ALU.add).then_inc(sem("mean_n4"), 1)
            dve.wait_ge(sem("root_n4"), 1)
            do(V.reciprocal(st[:, 4, 0:6], st[:, 7, 0:6]))
            for k in range(KT):
                TS(xn3[:, k], res[:, k], st[:, 4, k:k + 1], None, ALU.mult).then_inc(sem("rows_n3"), 1)
            for k in range(2):
                TS(ctr[:, k], ctr[:, k], st[:, 4, 4 + k:5 + k], None, ALU.mult).then_inc(sem("rows_nc"), 1)
            do(V.memset(raw.rearrange("p b y x -> p (b y x)"), 0.0))
            V.memset(rawc.rearrange("p b x -> p (b x)"), 0.0).then_inc(sem("raw_zero"), 1)
            g = first_group["-gt"] + 2
            ps = bank(g)[:, 0:96].rearrange("p (c a h) -> p a c h", c=6, h=H)
            dve.wait_ge(sem("wg_loaded"), 48)
            for kind in range(2):
                for d in range(2):
                    ins = V.tensor_copy(gk[:, 7 + kind, d], ps[:, 2 * kind + d])
                    if kind and d:
                        ins.then_inc(sem("dve_evac"), 1)
                        evacuated(dve, g)
                    else:
                        do(ins)
            gkd = lambda n: gk[:, n]
            b48 = lambda n: gkb[:, n].rearrange("p (d h) -> p d h", d=2)
            for d in range(2):
                do(TT(gk[:, 8, d], gk[:, 8, d], b48(0)[:, d].unsqueeze(1).to_broadcast([P, 6, H]), ALU.add))
            STT(gkd(9), gkd(8), -1.0, gkd(8), ALU.mult, ALU.max).then_inc(sem("gate_in"), 1)
            dve.wait_ge(sem("gate_out"), 3)
            do(TS(gkd(BETA), gkd(10), 0.5, 0.5, ALU.mult, ALU.add))
            z, z2, s_ = gkd(9), gkd(10), gkd(12)
            do(TS(z, gkd(11), 2.0, None, ALU.add))
            do(V.reciprocal(z, z))
            do(TT(z, z, gkd(11), ALU.mult))
            do(TT(z2, z, z, ALU.mult))
            do(TS(s_, z2, 1 / 15., None, ALU.mult))
            for c in (13., 11., 9., 7., 5., 3.):
                do(STT(s_, s_, 1 / c, z2, ALU.add, ALU.mult))
            do(STT(s_, s_, 1.0, z, ALU.add, ALU.mult))
            do(TS(gkd(8), gkd(8), 0.0, None, ALU.max))
            do(STT(s_, s_, 2.0, gkd(8), ALU.mult, ALU.add))
            for d in range(2):
                ins = STT(gk[:, G, d], s_[:, d], -1.0, b48(1)[:, d].unsqueeze(1).to_broadcast([P, 6, H]), ALU.mult, ALU.mult)
                if d:
                    ins.then_inc(sem("g_ready"), 1)
                    dve.wait_ge(sem("g_ready"), 1)
                else:
                    do(ins)

            def taps(n):
                name, i, _, r0 = conv_jobs[n]
                evacuated(dve, first_group[name] + i)
                if n >= 2:
                    dve.wait_ge(sem("qkv_ready"), n - 1)
                grid = i < 4
                r = r0 + i % 4
                if grid:
                    o = cbuf[:, n % 2].rearrange("p (y x) -> p y x", y=8)
                    shifts = [(3 * y + x, raw[:, n % 2, y:y + 8, x:x + 64]) for y in range(3) for x in range(3)]
                else:
                    o = cbuf[:, n % 2, 0:TC]
                    shifts = [(3 + x, rawc[:, n % 2, x:x + TC]) for x in range(3)]
                for m, (k, v) in enumerate(shifts):
                    w = col(1, 8 + 12 * k + r)
                    ins = TS(o, v, w, None, ALU.mult) if m == 0 else STT(o, v, w, o, ALU.mult, ALU.add)
                    if m == len(shifts) - 1:
                        ins.then_inc(sem("taps_done"), 1)
                    else:
                        do(ins)

            def silu(n):
                name, i, dst, _ = conv_jobs[n]
                w = T if i < 4 else TC
                dve.wait_ge(sem("taps_tanh"), n + 1)
                STT(dst[:, i % 4], tbuf[:, n % 2, 0:w], 1.0, cbuf[:, n % 2, 0:w], ALU.add, ALU.mult).then_inc(
                    sem("qkv_ready"), 1)

            for n in range(20):
                taps(n)
                if n:
                    silu(n - 1)
            dve.wait_ge(sem("g_sums"), 1)
            do(V.tensor_copy(gkd(GCUM), PB[4][:, 0:48].rearrange("p (d c h) -> p d c h", d=2, c=6)))
            do(V.tensor_copy(gkd(ETOT), PB[4][:, 48:96].rearrange("p (d c h) -> p d c h", d=2, c=6)))
            TT(gkd(12), gkd(ETOT), gkd(GCUM), ALU.subtract).then_inc(sem("gdiff"), 1)
            silu(19)
            dve.wait_ge(sem("gexp"), 3)
            do(TS(gkd(NEG), gkd(EG), -1.0, None, ALU.mult))
            for c in range(4):
                g = first_group["iz"] + c
                dve.wait_ge(sem("z_tanh"), c + 1)
                STT(zT[:, c], tbuf[:, c % 2], 1.0, bank(g)[:], ALU.add, ALU.mult).then_inc(sem("dve_evac"), 1)
            g0 = first_group["-ss"]
            for m, (t, i, s, w) in enumerate(norm_jobs):
                evacuated(dve, g0 + m)
                do(V.reciprocal(rtb[:, m % 2, 0:w], rtb[:, m % 2, 0:w]))
                STT(t[:, i], rtb[:, m % 2, 0:w], s, t[:, i], ALU.mult, ALU.mult).then_inc(sem("normed"), 1)
            for c in range(6):
                g = first_group["-tk"] + 2 * c + 1
                TS(vtok[:, c].rearrange("p h d -> p (h d)"), bank(g)[:], 0.5, None, ALU.mult).then_inc(sem("dve_evac"), 1)
            evacuated(dve, last_group["-tk"] - 1)
            evacuated(dve, last_group["-tk"] - 2)
            do(V.memset(S.rearrange("p d h e -> p (d h e)"), 0.0))
            V.memset(zero, 0.0).then_inc(sem("zero_ready"), 1)
            for n in range(12):
                dve_delta(dve, ch, do, n)
            of = oacc.rearrange("p k h d -> p (k h) d")
            sq = at(144, 8).rearrange("p (a d) -> p a d", a=16)
            do(TT(sq, of, of, ALU.mult))
            V.tensor_reduce(osq[:, 32:48], sq, AXX, ALU.add).then_inc(sem("o_sum"), 1)
            dve.wait_ge(sem("o_sum"), 1)
            TS(osq[:, 0:16], osq[:, 32:48], 1.0 / P, EPS, ALU.mult, ALU.add).then_inc(sem("o_mean"), 1)
            dve.wait_ge(sem("o_root"), 1)
            do(V.reciprocal(osq[:, 32:48], osq[:, 16:32]))
            do(TS(osq[:, 32:48], osq[:, 32:48], 0.5, None, ALU.mult))
            TT(of, of, osq[:, 32:48].unsqueeze(2).to_broadcast([P, 16, P]), ALU.mult).then_inc(sem("o_ready"), 1)
            for h in range(H):
                g = first_group["-ot"] + h
                STT(mixO[:, h], bank(g)[:], col(1, 124), zT[:, h], ALU.mult, ALU.mult).then_inc(sem("dve_evac"), 1)
            for h in range(2):
                for k in range(KT):
                    g = first_group[f"wp{h}"] + k
                    c = slice(512 * h, 512 * h + 512)
                    TT(at(120 + 2 * (k % 2), 2), bank(g)[:], modb[:, c], ALU.mult).then_inc(sem("dve_evac"), 1)
                    evacuated(dve, g)
                    TT(res[:, k, c], res[:, k, c], at(120 + 2 * (k % 2), 2), ALU.add).then_inc(sem("x2_ready"), 1)
            dve_moe(dve, ch, do, bank)

        def dve_delta(dve, ch, do, n):
            V = nc.vector
            TT, TS, STT = V.tensor_tensor, V.tensor_scalar, V.scalar_tensor_tensor
            d, c = batches[n]
            lat = c < 4
            heads = lambda row: gk[:, row, d, c].unsqueeze(2).to_broadcast([P, H, P])
            mask = lambda name: C[name].unsqueeze(1).to_broadcast([P, H, P])
            ps = lambda b: V4(PB[b][:])
            E4 = V4(E)
            if n == 0:
                dve_row(dve, do, 0)
            do(TT(V4(KD_), ktok[:, c], heads(KDEC), ALU.mult))
            dve.wait_ge(sem("d_row"), n + 1)
            do(TT(E4, ps(2), heads(GCUM), ALU.subtract))
            TS(E, E, 0.0, None, ALU.min).then_inc(sem("d_diff"), 1)
            dve.wait_ge(sem("d_kk"), n + 1)
            do(TT(V4(MU), ps(0), heads(BETA), ALU.mult))
            dve.wait_ge(sem("d_exp"), n + 1)
            do(TT(E4, E4, mask(("up", "lo")[d]), ALU.mult))
            if lat:
                dve.wait_ge(sem("d_kq"), sum(b[1] < 4 for b in batches[:n + 1]))
                do(TT(V4(AT), ps(1), E4, ALU.mult))
            do(TT(MU, MU, E, ALU.mult))
            TT(V4(MU), V4(MU), mask(("up_s", "lo_s")[d]), ALU.mult).then_inc(sem("d_mu"), 1)
            dve.wait_ge(sem("d_mu"), n + 1)
            mask2 = lambda name: C[name].unsqueeze(1).to_broadcast([P, 2, P])

            def base(u, src):
                for f in range(2):
                    TT(NX[:, f, u], src[:, 2 * f:2 * f + 2], mask2("bd16"), ALU.mult).then_inc(sem("d_n"), 1)
                for f in range(2):
                    dve.wait_ge(sem("d_n"), 4 * n + 2 * u_order[u] + f + 1)
                    STT(TX[:, f, u], NX[:, f, u], -1.0, mask2("ident"), ALU.mult, ALU.add).then_inc(sem("d_base"), 1)

            u_order = {UP: 0, LO: 1}
            base(UP, V4(MU))
            dve.wait_ge(sem("d_mt"), n + 1)
            base(LO, ps(3))
            TT(V4(MS[0]), V4(MU), mask("lv16"), ALU.mult).then_inc(sem("d_ms"), 1)
            TT(V4(MS[1]), V4(MU), mask("lv32"), ALU.mult).then_inc(sem("d_ms"), 1)

            def update(r, f, op):
                dve.wait_ge(sem("d_up"), 12 * n + 2 * r + f + 1)
                if r < 5:
                    TT(half(TX, f), half(TX, f), PB[4 + f][:], op).then_inc(sem("d_upc"), 1)
                else:
                    t = TX[:, f, UP].rearrange("p h i -> p (h i)")
                    TT(t, t, PB[4 + f][:, 256:512], op).then_inc(sem("d_upc"), 1)

            dve.wait_ge(sem("d_base"), 4 * n + 4)
            update(0, 0, ALU.add)
            update(0, 1, ALU.add)
            dve.wait_ge(sem("d_ks"), n + 1)
            do(TT(V4(TMP), ps(0), heads(NEG), ALU.mult))
            TT(V4(R_), V4(TMP), vtok[:, c], ALU.add).then_inc(sem("d_r"), 1)
            update(1, 0, ALU.add)
            update(1, 1, ALU.add)
            if lat:
                dve.wait_ge(sem("d_qs"), sum(b[1] < 4 for b in batches[:n + 1]))
                dve.wait_ge(sem("d_r"), n + 1)
                do(TT(V4(TMP), ps(1), heads(EG), ALU.mult))
            TT(S[:, d], S[:, d], heads(ETOT), ALU.mult).then_inc(sem("d_state"), 1)
            update(2, 0, ALU.add)
            update(2, 1, ALU.add)
            for r in range(3, 6):
                update(r, 0, ALU.subtract)
                update(r, 1, ALU.subtract)
                if r == 3:
                    TT(V4(MS[0]), V4(MU), mask("lv64"), ALU.mult).then_inc(sem("d_ms"), 1)
            dve.wait_ge(sem("d_v"), n + 1)
            TT(V4(VN), ps(2), heads(BETA), ALU.mult).then_inc(sem("d_vn"), 1)
            if n + 1 < 12:
                dve_row(dve, do, n + 1)
            dve.wait_ge(sem("d_state"), n + 1)
            dve.wait_ge(sem("d_su"), n + 1)
            TT(S[:, d], S[:, d], ps(6), ALU.add).then_inc(sem("d_s"), 1)
            dve.wait_ge(sem("d_s"), n + 1)
            if lat:
                first = not any(b[1] == c for b in batches[:n])
                dve.wait_ge(sem("d_o"), sum(b[1] < 4 for b in batches[:n + 1]))
                if first:
                    TT(oacc[:, c], V4(TMP), ps(3), ALU.add).then_inc(sem("batch_done"), 1)
                else:
                    do(TT(V4(TMP), V4(TMP), ps(3), ALU.add))
                    TT(oacc[:, c], oacc[:, c], V4(TMP), ALU.add).then_inc(sem("batch_done"), 1)
                dve.wait_ge(sem("batch_done"), n + 1)
            else:
                V.tensor_copy(TMP[:, 0:1], S[:, d, 0, 0:1]).then_inc(sem("batch_done"), 1)
                dve.wait_ge(sem("batch_done"), n + 1)

        def dve_row(dve, do, n):
            d, c = batches[n]
            for h in range(H):
                nc.vector.tensor_scalar(V4(GR)[:, h], C[("up", "lo")[d]], gk[:, G, d, c, h:h + 1], None,
                                        ALU.mult).then_inc(sem("d_grh" if h < H - 1 else "d_gr"), 1)

        PAIRS = NE // 2

        def over_pairs(eng, step):
            step(0, True, False)
            with eng.Fori(1, PAIRS - 1) as i:
                step(i, False, False)
            step(PAIRS - 1, False, True)

        def over_overflow(eng, step):
            eng.wait_ge(sem("ovi_ready"), 1)
            count = eng.value_load(ovi[0:1, 16:17], min_val=0, max_val=NOV)
            with eng.Fori(0, NOV) as b:
                with eng.If(b < count):
                    step(b)
            return count


        def sp_experts(sp):
            def load(s, e, n, wait):
                one = lambda w: (a[w][0][e] if isinstance(e, int) else a[w][0][bass.ds(e, 1)].rearrange(
                    "o d n -> (o d) n")).rearrange("(k p) n -> p k n", p=P)
                if wait:
                    sp.wait_ge(sem("e_gu"), n)
                sp.dma_start(GU[s][:, 0], one("w_gate_2")).then_inc(sem(f"gu_loaded{s}"), 16)
                sp.dma_start(GU[s][:, 1], one("w_up_2")).then_inc(sem(f"gu_loaded{s}"), 16)
                if wait:
                    sp.wait_ge(sem("e_down"), n)
                sp.dma_start(WD[s], one("w_down_2")).then_inc(sem(f"down_loaded{s}"), 16)

            first = lambda w, e: a[w][0][e].rearrange("(k p) n -> p k n", p=P)
            sp.wait_ge(sem("group_done"), last_group["dft"])
            sp.dma_start(GU[0][:, 1], first("w_up_2", 0)).then_inc(sem("gu_loaded0"), 16)
            sp.wait_ge(sem("batch_done"), 12)
            sp.dma_start(GU[0][:, 0], first("w_gate_2", 0)).then_inc(sem("gu_loaded0"), 16)
            sp.wait_ge(sem("group_done"), last_group["wp0"])
            sp.dma_start(WD[0], first("w_down_2", 0)).then_inc(sem("down_loaded0"), 16)
            sp.wait_ge(sem("x2_ready"), 8)
            sp.dma_start(GU[1][:, 1], first("w_up_2", 1)).then_inc(sem("gu_loaded1"), 16)
            sp.dma_start(WD[1], first("w_down_2", 1)).then_inc(sem("down_loaded1"), 16)
            sp.wait_ge(sem("group_done"), first_group["-lg"] + 1)
            sp.dma_start(GU[1][:, 0], first("w_gate_2", 1)).then_inc(sem("gu_loaded1"), 16)

            def pair(i, first, last):
                if not first:
                    for s in range(2):
                        load(s, 2 * i + s, 2 * i + s - 1, True)

            over_pairs(sp, pair)

            def overflow(b):
                e = sp.value_load(ovi[0:1, bass.ds(b, 1)], min_val=0, max_val=NE - 1)
                load(0, e, b + NE, True)

            over_overflow(sp, overflow)
            sp.wait_ge(sem("x3_ready"), KT)
            sp.dma_start(out[0].rearrange("(k p) d -> p k d", p=P), res).then_inc(sem("out_written"), 16)
            sp.wait_ge(sem("out_written"), 16)

        def pool_experts(pool):
            pool.wait_ge(sem("zero_ready"), 1)
            pool.dma_start(xs.rearrange("(r p) d -> p r d", p=P),
                           zero.unsqueeze(1).to_broadcast([P, CAP * (NE + NOV + 1) // P, D])).then_inc(sem("xs_zeroed"), 16)
            pool.dma_start(ys[CAP * NE:].rearrange("(r p) d -> p r d", p=P),
                           zero.unsqueeze(1).to_broadcast([P, CAP * (NOV + 1) // P, D])).then_inc(sem("xs_zeroed"), 16)
            pool.wait_ge(sem("xs_zeroed"), 32)
            pool.wait_ge(sem("xm_ready"), KT)
            pool.wait_ge(sem("idx_ready"), 1)
            for r in range(2):
                for k in range(KT):
                    pool.indirect_dma_start(xs, bass.IndirectOffsetOnAxis(ap=idx[:, r, k:k + 1], axis=0), xm[:, k], None).then_inc(
                        sem("scattered"), 16)
            pool.wait_ge(sem("scattered"), 16 * 2 * KT)

            def rows_of(t, n, h):
                r = t[CAP * n:CAP * n + CAP] if isinstance(n, int) else t[bass.ds(n * CAP, CAP)]
                return r[:, 512 * h:512 * h + 512]

            def pause(n):
                if not isinstance(n, int) or n:
                    pool.wait_ge(sem("pool_pad"), n)
                nc.gpsimd.tensor_tensor(pad[:], ident[:, 0:1], ident[:, 0:1], ALU.mult).then_inc(sem("pool_pad"), 1)

            def load(s, n, wait, pauses=0):
                if wait is not None:
                    pool.wait_ge(sem("e_turn"), wait)
                    pause(pauses)
                for h in range(2):
                    pool.dma_start(XE[s][64 * h:64 * h + 64], rows_of(xs, n, h)).then_inc(sem(f"xe_loaded{s}"), 16)

            def store(s, n, pauses):
                pool.wait_ge(sem("e_copied"), n + 1)
                pause(pauses)
                for h in range(2):
                    pool.dma_start(rows_of(ys, n, h), YO[s][64 * h:64 * h + 64]).then_inc(sem(f"ys_written{s}"), 16)

            load(0, 0, None)
            load(1, 1, None)

            def pair(i, first, last):
                for s in range(2):
                    if not last:
                        load(s, 2 * i + s + 2, 2 * i + s + 1, 4 * i + 2 * s)
                    store(s, 2 * i + s, 4 * i + (s if last else 2 * s + 1))

            over_pairs(pool, pair)

            def overflow(b):
                load(0, b + NE, b + NE, 2 * b + 4 * PAIRS - 2)
                store(0, b + NE, 2 * b + 4 * PAIRS - 1)

            count = over_overflow(pool, overflow)
            pool.wait_ge(sem("ys_written0"), count * 32 + 32 * PAIRS)
            pause(count * 2 + 4 * PAIRS - 2)
            pool.wait_ge(sem("ys_written1"), 32 * PAIRS)
            pool.wait_ge(sem("e_down"), NE)
            for k in range(KT):
                for r in range(2):
                    pool.indirect_dma_start(YG[:, r, k], None, ys, bass.IndirectOffsetOnAxis(ap=idx[:, r, k:k + 1], axis=0)).then_inc(
                        sem(f"gathered{k}"), 16)

        def pe_router(pe):
            pe.wait_ge(sem("xm_ready"), KT)
            pe_turn(pe, xm, KT, "n5")
            unit_evacuated(pe, "-n5")
            pe.wait_ge(sem("wr_loaded"), 64)
            g = first_group["-lg"]
            pe_group(pe, g, PB[g % 4][0:36, :], [wr[:, k] for k in range(KD)], [xT[:, k] for k in range(KD)])
            evacuated(pe, g)
            evacuated(pe, g - 3)
            for k in range(KT):
                l = nc.tensor.transpose(PB[(g + 1) % 4][:, 36 * k:36 * k + 36], lgT[0:36, k * P:(k + 1) * P], ident[0:36, 0:36])
            l.then_inc(sem("group_done"), 1)
            pe.wait_ge(sem("chosen"), 1)
            g = first_group["-cn"]
            both = rt(5)
            for k in range(KT + 1):
                o = PB[g % 4][:, NE * k:NE * k + NE]
                for j in range(min(k + 1, KT)):
                    l = nc.tensor.matmul(o, C["up_s"] if j == k else ones, both[:, j], start=(j == 0),
                                         stop=(j == min(k, KT - 1)))
            l.then_inc(sem("group_done"), 1)

        def pe_experts(pe):
            def turn(s, n, m, wait):
                pe.wait_ge(sem(f"xe_loaded{s}"), m * 32 + 32)
                if wait is not None:
                    pe.wait_ge(sem("e_xg"), wait)
                for c in range(4):
                    l = nc.tensor.transpose(PB[s][:, c * P:(c + 1) * P], XE[s][:, c * P:(c + 1) * P], ident)
                l.then_inc(sem("e_turn"), 1)

            def block(s, n, m, wait, next_turn):
                pe.wait_ge(sem(f"gu_loaded{s}"), m * 32 + 32)
                pe.wait_ge(sem("e_xg"), n + 1)
                if wait is not None:
                    pe.wait_ge(sem("e_hid"), wait)
                for k in range(KD):
                    for h in range(2):
                        l = nc.tensor.matmul(PB[2 + s][64 * h:64 * h + 64, :].rearrange("p (g n) -> p g n", g=2),
                                             XG[s][:, k % 4, 64 * (k // 4):64 * (k // 4) + 64],
                                             GU[s][:, :, k, 256 * h:256 * h + 256], start=(k == 0), stop=(k == KD - 1))
                l.then_inc(sem("e_gu"), 1)
                if next_turn:
                    next_turn()
                pe.wait_ge(sem("e_hid"), n + 1)
                if wait is not None:
                    pe.wait_ge(sem("e_htc"), wait)
                for c in range(2):
                    l = nc.tensor.transpose(PB[4 + s][:, c * P:(c + 1) * P], HB[s][:, c * P:(c + 1) * P], ident)
                l.then_inc(sem("e_ht"), 1)
                pe.wait_ge(sem(f"down_loaded{s}"), m * 16 + 16)
                pe.wait_ge(sem("e_htc"), n + 1)
                if wait is not None:
                    pe.wait_ge(sem("e_copied"), wait)
                for j in range(4):
                    for h in range(2):
                        l = nc.tensor.matmul(PB[6 + s][64 * h:64 * h + 64, :], HT[s][:, j % 2, 64 * (j // 2):64 * (j // 2) + 64],
                                             WD[s][:, j, 512 * h:512 * h + 512], start=(j == 0), stop=(j == 3))
                l.then_inc(sem("e_down"), 1)

            unit_evacuated(pe, "-cn")
            evacuated(pe, first_group["-lg"] + 1)
            turn(0, 0, 0, None)

            def pair(i, first, last):
                n = 2 * i
                block(0, n, i, None if first else n - 1, lambda: turn(1, n + 1, i, None if first else n))
                block(1, n + 1, i, None if first else n,
                      None if last else lambda: turn(0, n + 2, i + 1, n + 1))

            over_pairs(pe, pair)

            def overflow(b):
                turn(0, b + NE, b + PAIRS, b + NE)
                block(0, b + NE, b + PAIRS, b + NE, None)

            over_overflow(pe, overflow)

        def act_experts(act):
            def block(s, n, m, wait):
                act.wait_ge(sem("e_gu"), n + 1)
                if wait is not None:
                    act.wait_ge(sem("e_hid"), wait)
                nc.scalar.activation(TB[s], PB[2 + s][:, 0:256], ACT.Tanh, scale=0.5).then_inc(sem("e_tanh"), 1)
                act.wait_ge(sem("e_ht"), n + 1)
                if wait is not None:
                    act.wait_ge(sem("e_down"), wait)
                nc.scalar.activation(HT[s].rearrange("p c n -> p (c n)"), PB[4 + s][:, 0:256], ACT.Copy).then_inc(
                    sem("e_htc"), 1)
                act.wait_ge(sem("e_down"), n + 1)
                if wait is not None:
                    act.wait_ge(sem(f"ys_written{s}"), m * 32)
                nc.scalar.activation(YO[s], PB[6 + s][:], ACT.Copy).then_inc(sem("e_copied"), 1)

            def pair(i, first, last):
                for s in range(2):
                    block(s, 2 * i + s, i, None if first else 2 * i + s - 1)

            over_pairs(act, pair)
            over_overflow(act, lambda b: block(0, b + NE, b + PAIRS, b + NE))

        def dve_experts(dve):
            STT = nc.vector.scalar_tensor_tensor

            def copy(s, n, wait):
                dve.wait_ge(sem("e_turn"), n + 1)
                if wait is not None:
                    dve.wait_ge(sem("e_gu"), wait)
                nc.vector.tensor_copy(XG[s].rearrange("p c n -> p (c n)"), PB[s][:]).then_inc(sem("e_xg"), 1)

            def hidden(s, n, wait):
                dve.wait_ge(sem("e_tanh"), n + 1)
                STT(SB[s], TB[s], 1.0, PB[2 + s][:, 0:256], ALU.add, ALU.mult).then_inc(sem("e_silu"), 1)
                dve.wait_ge(sem("e_silu"), n + 1)
                if wait is not None:
                    dve.wait_ge(sem("e_ht"), wait)
                STT(HB[s], SB[s], 0.5, PB[2 + s][:, 256:512], ALU.mult, ALU.mult).then_inc(sem("e_hid"), 1)

            copy(0, 0, None)

            def pair(i, first, last):
                n = 2 * i
                copy(1, n + 1, None if first else n)
                hidden(0, n, None if first else n - 1)
                if not last:
                    copy(0, n + 2, n + 1)
                hidden(1, n + 1, None if first else n)

            over_pairs(dve, pair)

            def overflow(b):
                copy(0, b + NE, b + NE)
                hidden(0, b + NE, b + NE)

            over_overflow(dve, overflow)

        def act_moe(act):
            act.wait_ge(sem("batch_done"), 12)
            act.wait_ge(sem("xs_zeroed"), 32)
            wr_src = lambda w: a[w][0].rearrange("(k p) n -> p k n", p=P)
            act.dma_start(wr[:, :, 0:4], wr_src("w_group_2")).then_inc(sem("wr_loaded"), 16)
            act.dma_start(wr[:, :, 4:36], wr_src("w_router_2")).then_inc(sem("wr_loaded"), 16)
            act.dma_start(rb[:, 0:4], a["b_group_2"].to_broadcast([P, 4])).then_inc(sem("wr_loaded"), 16)
            act.dma_start(rb[:, 4:36], a["b_router_2"].to_broadcast([P, NE])).then_inc(sem("wr_loaded"), 16)
            act.dma_start(fgb, a["final_g_2"].rearrange("(o d) -> o d", o=1).to_broadcast([P, D])).then_inc(
                sem("fgb_loaded"), 16)
            for k in range(KT):
                act.wait_ge(sem("x2_ready"), 5 + k)
                nc.scalar.activation(at(156, 4), res[:, k], ACT.Square, accum_out=st[:, 0, k:k + 1]).then_inc(
                    sem("squares_n5"), 1)
                act.wait_ge(sem("squares_n5"), k + 1)
            act_root(act, KT, "n5")
            act_turned(act, xT, KT, "n5", lambda c: 1.0)
            g = first_group["-lg"]
            act.wait_ge(sem("group_done"), g + 1)
            nc.scalar.activation(lgT[0:36, :], PB[g % 4][0:36, :], ACT.Copy).then_inc(sem("act_evac"), 1)
            act.wait_ge(sem("g_in"), 1)
            nc.scalar.activation(rt(4, 4), rt(3, 4), ACT.Exp).then_inc(sem("g_exp"), 1)
            act.wait_ge(sem("e2_in"), 1)
            nc.scalar.activation(tk[:, 6], tk[:, 5], ACT.Exp).then_inc(sem("e2_exp"), 1)
            act_experts(act)
            for k in range(KT):
                act.wait_ge(sem("x3_sum"), k + 1)
                nc.scalar.activation(at(48, 4), res[:, k], ACT.Square, accum_out=st[:, 0, k:k + 1]).then_inc(
                    sem("squares_n6"), 1)
                act.wait_ge(sem("squares_n6"), k + 1)
            act_root(act, KT, "n6")

        def dve_moe(dve, ch, do, bank):
            V = nc.vector
            TT, TS, STT = V.tensor_tensor, V.tensor_scalar, V.scalar_tensor_tensor
            dve_rstd(dve, ch, KT, D, "n5")
            for k in range(KT):
                do(STT(xm[:, k], res[:, k], st[:, 4, k:k + 1], modb[:, 2048:3072], ALU.mult, ALU.mult))
                TT(xm[:, k], xm[:, k], modb[:, 1024:2048], ALU.add).then_inc(sem("xm_ready"), 1)
            g = first_group["-lg"] + 1
            dve.wait_ge(sem("wr_loaded"), 64)
            lg = at(144, 8)[:, 0:144].rearrange("p (k n) -> p k n", k=KT)
            TT(lg, bank(g)[:, 0:144].rearrange("p (k n) -> p k n", k=KT), rb.unsqueeze(1).to_broadcast([P, KT, 36]),
               ALU.add).then_inc(sem("dve_evac"), 1)
            evacuated(dve, g)
            over = lambda x, n: x.unsqueeze(2).to_broadcast([P, KT, n])
            row = lambda name, n: C[name].unsqueeze(1).to_broadcast([P, KT, n])
            T_ = lambda n: tk[:, n]

            def first_max(x, best, names, n, eq, at_, hot):
                do(V.tensor_reduce(best, x, AXX, ALU.max))
                do(TT(eq, x, over(best, n), ALU.is_ge))
                do(STT(eq, eq, -64.0, row(names, n), ALU.mult, ALU.add))
                do(V.tensor_reduce(at_, eq, AXX, ALU.min))
                do(TS(at_, at_, 64.0, None, ALU.add))
                do(TT(hot, row(names, n), over(at_, n), ALU.is_equal))

            gl, el = lg[:, :, 0:4], lg[:, :, 4:36]
            eqg, hotg = rt(2, 4), rt(6, 4)
            first_max(gl, T_(0), "gidx", 4, eqg, T_(1), hotg)
            TT(rt(3, 4), gl, over(T_(0), 4), ALU.subtract).then_inc(sem("g_in"), 1)
            dve.wait_ge(sem("g_exp"), 1)
            do(V.tensor_reduce(T_(2), rt(4, 4), AXX, ALU.add))
            do(V.reciprocal(T_(2), T_(2)))
            do(TS(eqg, hotg, 1e30, -1e30, ALU.mult, ALU.add))
            elm, eq, hot1, hot2, both = rt(3), rt(4), rt(7), rt(8), rt(5)
            do(TT(elm.rearrange("p k (g e) -> p k g e", g=4), el.rearrange("p k (g e) -> p k g e", g=4),
                  eqg.unsqueeze(3).to_broadcast([P, KT, 4, 8]), ALU.add))
            first_max(elm, T_(3), "eidx", NE, eq, T_(7), hot1)
            do(STT(elm, hot1, -1e30, elm, ALU.mult, ALU.add))
            first_max(elm, T_(4), "eidx", NE, eq, T_(8), hot2)
            TT(both, hot1, hot2, ALU.add).then_inc(sem("chosen"), 1)
            TT(T_(5), T_(4), T_(3), ALU.subtract).then_inc(sem("e2_in"), 1)
            dve.wait_ge(sem("e2_exp"), 1)
            do(TS(T_(9), T_(6), 1.0, None, ALU.add))
            do(V.reciprocal(T_(9), T_(9)))
            do(TT(T_(10), T_(2), T_(9), ALU.mult))
            do(TT(T_(11), T_(10), T_(6), ALU.mult))
            g = first_group["-cn"]
            cnt = at(144, 8)[:, P * 9:P * 9 + 160]
            V.tensor_copy(cnt, bank(g)[:, 0:160]).then_inc(sem("dve_evac"), 1)
            evacuated(dve, g)
            before = cnt[:, 0:P].rearrange("p (k e) -> p k e", k=KT)
            tot = cnt[:, P:P + NE]
            w32 = lambda n: at(144, 8)[:, P * 11 + NE * n:P * 11 + NE * n + NE]
            nb, oend, obase = w32(0), w32(1), w32(2)
            do(TS(nb, tot, float(CAP), None, ALU.is_gt))
            for j in range(2, T // CAP):
                do(STT(nb, tot, float(CAP * j), nb, ALU.is_gt, ALU.add))
            do(V.tensor_tensor_scan(oend, ones[:, 0:NE], nb, 0.0, ALU.mult, ALU.add))
            do(TT(obase, oend, nb, ALU.subtract))
            do(TS(obase, obase, float(CAP), float(CAP * (NE - 1)), ALU.mult, ALU.add))
            for r, hot in enumerate((hot1, hot2)):
                for j, v in enumerate((before, row("e64", NE), obase.unsqueeze(1).to_broadcast([P, KT, NE]))):
                    do(TT(eq, hot, v, ALU.mult))
                    do(V.tensor_reduce(T_(12 + j), eq, AXX, ALU.add))
                do(TS(T_(15), T_(12), float(CAP), None, ALU.is_lt))
                do(TT(T_(13), T_(13), T_(14), ALU.subtract))
                do(TT(T_(13), T_(13), T_(15), ALU.mult))
                do(TT(T_(13), T_(13), T_(14), ALU.add))
                do(TT(T_(13), T_(13), T_(12), ALU.add))
                do(V.tensor_copy(idx[:, r], T_(13)))
            V.tensor_copy(tk[:, 16], T_(13)).then_inc(sem("idx_ready"), 1)
            cmp_ = at(152, 2).rearrange("p (b e) -> p b e", b=16)
            do(TT(cmp_, oend.unsqueeze(1).to_broadcast([P, 16, NE]), C["blk"].unsqueeze(2).to_broadcast([P, 16, NE]),
                  ALU.is_le))
            do(V.tensor_reduce(w32(3)[:, 0:16], cmp_, AXX, ALU.add))
            do(TS(w32(3)[:, 0:16], w32(3)[:, 0:16], float(NE - 1), None, ALU.min))
            do(V.tensor_copy(w32(3)[:, 16:17], oend[:, NE - 1:NE]))
            V.tensor_copy(ovi[:], w32(3)[:, 0:17]).then_inc(sem("ovi_ready"), 1)
            dve.wait_ge(sem("ovi_ready"), 1)
            dve_experts(dve)
            for k in range(KT):
                dve.wait_ge(sem(f"gathered{k}"), 32)
                y1, y2 = YG[:, 0, k], YG[:, 1, k]
                do(TS(y1, y1, tk[:, 10, k:k + 1], None, ALU.mult))
                do(STT(y1, y2, tk[:, 11, k:k + 1], y1, ALU.mult, ALU.add))
                do(TT(y1, y1, modb[:, 3072:4096], ALU.mult))
                TT(res[:, k], res[:, k], y1, ALU.add).then_inc(sem("x3_sum"), 1)
            dve_rstd(dve, ch, KT, D, "n6")
            dve.wait_ge(sem("fgb_loaded"), 16)
            for k in range(KT):
                STT(res[:, k], res[:, k], st[:, 4, k:k + 1], fgb, ALU.mult, ALU.mult).then_inc(sem("x3_ready"), 1)

        @block.sync
        def _(sp):
            sp.dma_start(res, a["x"][0].rearrange("(k p) d -> p k d", p=P)).then_inc(sem("x_loaded"), 16)
            sp.dma_start(cst[:], a["consts"]).then_inc(sem("consts_loaded"), 16)
            for n, name in enumerate(names):
                if n >= RSLOTS:
                    freed(sp, names[n - RSLOTS])
                if name == "wo0":
                    sp.wait_ge(sem("y_done"), NJ)
                    sp.dma_start(res, a["x"][0].rearrange("(k p) d -> p k d", p=P)).then_inc(sem("x_back"), 16)
                dst, src = unit_view(name)
                sp.dma_start(dst, src).then_inc(sem(f"unit_loaded{n % RSLOTS}"), 16)
            sp_experts(sp)

        @block.tensor
        def _(pe):
            pe.wait_ge(sem("consts_loaded"), 16)
            pe.wait_ge(sem("rows_loaded"), 16 * N_ROWS)
            for t, n in enumerate((120, 125, 32)):
                l = nc.tensor.transpose(PB[7][:, t * P:t * P + n], rows[0:n, t, :], ident[0:n, 0:n])
            l.then_inc(sem("cols_turned"), 1)
            pe.wait_ge(sem("ldt_spread"), 1)
            nc.tensor.transpose(PB[7][:, 384:384 + NJ], ldtr[:], ident[0:NJ, 0:NJ]).then_inc(sem("cols_turned"), 1)
            pe.wait_ge(sem("rows_n1"), KT)
            pe_turn(pe, xn, KT, "n1")
            unit_evacuated(pe, "-n1")
            loaded(pe, "u")
            pe_unit_T(pe, "u", xT, KD)
            pe.wait_ge(sem("c_loaded"), 64)
            for r in range(2):
                for q in range(4):
                    l = nc.tensor.transpose(PB[4 + r][:, q * P:(q + 1) * P],
                                            cld[:, r, q].rearrange("p d n -> p (d n)"), ident)
            l.then_inc(sem("c_turned"), 1)
            pe.wait_ge(sem("bbd_ready"), 1)
            pe.wait_ge(sem("ldt_col"), 1)
            for r in range(2):
                for q in range(4):
                    l = nc.tensor.transpose(PB[6 + r][:, q * P:(q + 1) * P],
                                            bbd[:, r, 4 * q:4 * q + 4].rearrange("p j g c -> p (j g c)"), ident)
            l.then_inc(sem("bb_turned"), 1)

            def bu(j):
                if j == 0:
                    pe.wait_ge(sem("bbT_ready"), 2)
                    pe.wait_ge(sem("cbd_ready"), 1)
                    unit_evacuated(pe, "u")
                else:
                    pe.wait_ge(sem("bu_read"), j)
                q, r0 = j // 4, 32 * (j % 4)
                for r in range(2):
                    l = nc.tensor.matmul(PB[4 + r][:], bbT[r0:r0 + 32, q, r, :], U[r0:r0 + 32, q, :], start=True,
                                         stop=True, tile_position=(r0, 0))
                l.then_inc(sem("bu_done"), 1)

            def y(j):
                pe.wait_ge(sem("s_ready"), j + 1)
                if j % 4 == 0 and j >= 8:
                    pe.wait_ge(sem("y_read"), j // 4 - 1)
                r0 = 32 * (j % 4)
                sj = ssm_w[:, 4 + 2 * (j % 2):6 + 2 * (j % 2)]
                for r in range(2):
                    l = nc.tensor.matmul(PB[6 + j // 4 % 2][r0:r0 + 32, :], cbd[:, r, j].rearrange("p g c -> p (g c)"), sj[:, r],
                                         start=(r == 0), stop=(r == 1), tile_position=(0, r0))
                l.then_inc(sem("y_done"), 1)

            j = 0
            for name in ("cg0", "cv0", "bg0", "cg1", "cv1", "bg1", "gc0", "gc1"):
                loaded(pe, name)
                for m in range(0, 4, 2):
                    bu(j)
                    if j >= 2:
                        y(j - 2)
                    g0 = first_group[name]
                    for i in (m, m + 1):
                        pe_group(pe, g0 + i, PB[(g0 + i) % 4][:], [W[name][:, k, i * P:(i + 1) * P] for k in range(KD)],
                                 [xT[:, k, :] for k in range(KD)])
                    j += 1
            y(NJ - 2)
            unit_evacuated(pe, "bg1")
            for name in ("co0", "co1"):
                loaded(pe, name)
                pe_unit_T(pe, name, YB, KD)
                if name == "co0":
                    y(NJ - 1)
            for name in ("gs0", "gs1"):
                loaded(pe, name)
                pe_unit_T(pe, name, xT, KD)
            loaded(pe, "ga")
            loaded(pe, "gb")
            pe.wait_ge(sem("z_ready"), 4)
            g0 = first_group["gb"]
            for c in range(KD):
                for i, w in enumerate(("ga", "gb")):
                    g = g0 + 2 * c + i
                    pe_group(pe, g, PB[g % 4][:], [W[w][:, k, c * P:(c + 1) * P] for k in range(4)],
                             [U[:, k, :] for k in range(4)])
            pe.wait_ge(sem("merged"), KD)
            for name in ("wo0", "wo1"):
                loaded(pe, name)
                pe_unit_R(pe, name, GC, KD)
            pe.wait_ge(sem("rows_n2"), KT)
            pe_turn(pe, xn2, KT, "n2")
            unit_evacuated(pe, "-n2")
            for h in range(2):
                for q in range(4):
                    loaded(pe, f"f1_{h}{q}")
                    if h == 1 and q == 0:
                        pass
                    pe_unit_T(pe, f"f1_{h}{q}", xT, KD)
                unit_evacuated(pe, f"f1_{h}3")
                for q in range(4):
                    loaded(pe, f"f2_{h}{q}")
                    if (h, q) == (1, 3):
                        pe_mod(pe)
                    pe_unit_R(pe, f"f2_{h}{q}", H1, 16, 256)
            pe_second(pe)

        @block.scalar
        def _(act):
            act_loads(act)
            act.wait_ge(sem("x_loaded"), 16)
            act_squares(act, res, KT, at(136, 4), "n1")
            act_root(act, KT, "n1")
            act.wait_ge(sem("cols_turned"), 2)
            for t, n in enumerate((120, 125, 32)):
                nc.scalar.activation(c1[:, t, 0:n], PB[7][:, t * P:t * P + n], ACT.Copy).then_inc(sem("cols_ready"), 1)
            nc.scalar.activation(sm[:, 0], PB[7][:, 384:384 + NJ], ACT.Copy).then_inc(sem("ldt_col"), 1)
            act.wait_ge(sem("cols_ready"), 3)
            act_turned(act, xT, KT, "n1", lambda c: col(0, 76 + c))

            def group(g, dst, func=ACT.Identity, scale=1.0, bias=0.0):
                act.wait_ge(sem("group_done"), g + 1)
                nc.scalar.activation(dst, PB[g % 4][:], func, scale=scale, bias=bias).then_inc(sem("act_evac"), 1)

            for c in range(4):
                group(first_group["u"] + c, U[:, c, :], bias=b_in_col(c))
            act.wait_ge(sem("angles_ready"), 1)
            for i, (dst, src) in enumerate(((tab_h, 0), (tab_l, 256))):
                n = (16, 32)[i]
                for r in range(2):
                    s = ssm_w[:, 2 * (1 - r) + i, 0:NJ * n].rearrange("p (j n) -> p j n", j=NJ)
                    nc.scalar.activation(dst[:, r], s, ACT.Sin, scale=TWO_PI).then_inc(sem("tables_ready"), 1)
            for r in range(2):
                nc.scalar.activation(sm[:, 10 + r], sm[:, 8 + r], ACT.Sin, scale=TWO_PI).then_inc(sem("tables_ready"), 1)
            act.wait_ge(sem("bb_turned"), 1)
            for r in range(2):
                nc.scalar.activation(bbT[:, :, r, :], PB[6 + r][:].rearrange("p (q s) -> p q s", q=4),
                                     ACT.Copy).then_inc(sem("bbT_ready"), 1)
            def gelu(q):
                act.wait_ge(sem("gelu_in"), q + 1)
                nc.scalar.activation(gelu_b[:, 2], gelu_b[:, 1], ACT.Tanh, scale=0.7978845608028654).then_inc(
                    sem("gelu_tanh"), 1)

            def gate(name, c, dst, b0):
                group(first_group[name] + c, dst[:, 4 * int(name[2]) + c, :], ACT.Tanh, 0.5, bhalf[:, b0 + c:b0 + c + 1])

            for c in range(4):
                group(first_group["cg0"] + c, VT[:, c, :], bias=b_in_col(12 + c))
            for c in range(4):
                act.wait_ge(sem("conv_done"), c + 1)
                group(first_group["cg1"] + c, VT[:, c, :], bias=b_in_col(16 + c))
                if c == 1:
                    gelu(0)
            gelu(1)
            act.wait_ge(sem("bhalf_ready"), 1)
            for c in range(4):
                gate("gc0", c, GC, 36)
            for c in range(4):
                gate("gc1", c, GC, 40)
                if c == 1:
                    gelu(2)
            gelu(3)
            for name, b0 in (("gs0", 28), ("gs1", 32)):
                for c in range(4):
                    gate(name, c, YB, b0)
            g0 = first_group["gb"]
            for c in range(KD):
                if c >= 2:
                    evacuated(act, g0 + 2 * (c - 2))
                group(g0 + 2 * c + 1, at(104 + 2 * (c % 2), 2), ACT.Tanh, 0.25)
            act.wait_ge(sem("silu_in"), 1)
            nc.scalar.activation(sc[:, 1], c1[:, 2, 0:16], ACT.Tanh, scale=0.5).then_inc(sem("silu_tanh"), 1)
            for k in range(KT):
                evacuated(act, first_group["wo1"] + k)
                nc.scalar.activation(at(152, 4), res[:, k], ACT.Square, accum_out=st[:, 0, k:k + 1]).then_inc(
                    sem("squares_n2"), 1)
                act.wait_ge(sem("squares_n2"), k + 1)
            act_root(act, KT, "n2")
            act_turned(act, xT, KT, "n2", lambda c: col(1, c))
            act.dma_start(gfb, a["norm_final_g"].rearrange("(o d) -> o d", o=1).to_broadcast([P, D])).then_inc(
                sem("gfb_loaded"), 16)
            act.dma_start(n2g, a["norm2_g_2"].to_broadcast([P, D])).then_inc(sem("bmod_loaded"), 16)
            act.dma_start(modb, a["b_mod_2"][:, 2048:6144].to_broadcast([P, 4096])).then_inc(sem("bmod_loaded"), 16)
            act.dma_start(wg, a["w_in_2"][0][:, 2560:2576].rearrange("(k p) n -> p k n", p=P)).then_inc(sem("wg_loaded"), 16)
            act.dma_start(gkb[:, 0], a["dt_bias_2"].rearrange("o d h -> o (d h)").to_broadcast([P, 8])).then_inc(
                sem("wg_loaded"), 16)
            act.dma_start(gkb[:, 1], a["a_log_2"].rearrange("o d h -> o (d h)").to_broadcast([P, 8])).then_inc(
                sem("wg_loaded"), 16)
            relu = Count(sem("relu_done"))
            for h in range(2):
                for c in range(16):
                    g = first_group[f"f1_{h}{c // 4}"] + c % 4
                    act.wait_ge(sem("group_done"), g + 1)
                    relu.done(act, nc.scalar.activation(at(188 + 2 * (c % 2), 2), PB[g % 4][:], ACT.Relu))
                    nc.scalar.activation(H1[:, c], at(188 + 2 * (c % 2), 2), ACT.Square).then_inc(sem("act_evac"), 1)
            for k in range(KT):
                evacuated(act, first_group["f2_13"] + k)
                nc.scalar.activation(at(80, 4), res[:, k], ACT.Square, accum_out=st[:, 0, k:k + 1]).then_inc(
                    sem("squares_n3"), 1)
                act.wait_ge(sem("squares_n3"), k + 1)
            act_root(act, KT, "n3")
            act_second(act, group)

        @block.vector
        def _(dve):
            V = nc.vector
            ch = Count(sem("dve_step"))
            TT, TS, STT = V.tensor_tensor, V.tensor_scalar, V.scalar_tensor_tensor
            do = lambda ins: ch.done(dve, ins)
            V.memset(bbd[:], 0.0).then_inc(sem("blocks_zero"), 1)
            V.memset(cbd[:], 0.0).then_inc(sem("blocks_zero"), 1)
            dve.wait_ge(sem("rows_loaded"), 16 * N_ROWS)
            V.tensor_copy(ldtr[:].rearrange("j (g n) -> j g n", g=2), ldt[:].unsqueeze(2).to_broadcast([NJ, 2, NS])).then_inc(
                sem("ldt_spread"), 1)
            dve.wait_ge(sem("x_loaded"), 16)
            dve_rstd(dve, ch, KT, D, "n1")
            dve_scale_rows(dve, res, xn, KT, "n1")
            dve.wait_ge(sem("rows_n1"), KT)

            dve.wait_ge(sem("cols_ready"), 3)
            dve.wait_ge(sem("ldt_col"), 1)
            V.tensor_scalar(bhalf[:], c1[:, 0, 0:44], 0.5, None, ALU.mult).then_inc(sem("bhalf_ready"), 1)
            R = lambda n: sm[:, n]
            lr, li = c1[:, 0, 88:104], c1[:, 0, 104:120]

            def wrap(dst, x, t):
                do(TS(t, x, MAGIC, MAGIC, ALU.add, ALU.subtract))
                do(TT(dst, x, t, ALU.subtract))

            def exp(dst, x, z, k, r, p):
                do(TS(z, x, -87.0, 88.0, ALU.max, ALU.min))
                do(TS(k, z, 1.4426950408889634, MAGIC, ALU.mult, ALU.add))
                do(TS(k, k, MAGIC, None, ALU.subtract))
                do(STT(r, k, -0.693359375, z, ALU.mult, ALU.add))
                do(STT(r, k, 2.12194440e-4, r, ALU.mult, ALU.add))
                do(TS(p, r, 1 / 5040., None, ALU.mult))
                for c in (1 / 720., 1 / 120., 1 / 24., 1 / 6., 0.5, 1.0):
                    do(STT(p, p, c, r, ALU.add, ALU.mult))
                do(TS(k, k, 127.0, None, ALU.add))
                do(V.tensor_copy(smi[:], k))
                do(TS(smi[:], smi[:], 23, None, ALU.logical_shift_left))
                do(STT(p, p, 1.0, smi[:].bitcast(F32), ALU.add, ALU.mult))
                do(TS(z, x, -87.0, None, ALU.is_ge))
                do(TT(dst, p, z, ALU.mult))

            do(TS(R(1), R(0), 0.0, None, ALU.add))
            exp(R(2), R(1), R(20), R(21), R(22), R(23))
            do(TT(R(3), lr, R(2), ALU.mult))
            exp(R(4), R(3), R(20), R(21), R(22), R(23))
            do(TT(R(5), li, R(2), ALU.mult))
            do(TS(R(6), R(5), 0.15915494309189535, MAGIC, ALU.mult, ALU.add))
            do(TS(R(6), R(6), MAGIC, None, ALU.subtract))
            do(STT(R(7), R(6), -6.28125, R(5), ALU.mult, ALU.add))
            do(STT(R(7), R(6), -1.9350051879882812e-3, R(7), ALU.mult, ALU.add))
            do(STT(R(7), R(6), -3.0199159819e-7, R(7), ALU.mult, ALU.add))
            do(TS(R(7), R(7), 0.15915494309189535, None, ALU.mult))
            wrap(R(9), R(7), R(24))

            def quarter(dst, x, t):
                do(STT(t, x, -1.0, x, ALU.mult, ALU.max))
                do(TS(dst, t, -1.0, 0.25, ALU.mult, ALU.add))

            quarter(R(8), R(9), R(24))
            do(TS(R(12), R(9), 32.0, None, ALU.mult))
            wrap(R(12), R(12), R(24))
            for i, (n, f, tt) in enumerate(((16, R(12), "t_high"), (32, R(9), "t_low"))):
                v = lambda b: ssm_w[:, b, 0:NJ * n].rearrange("p (j n) -> p j n", j=NJ)
                do(TT(v(i), f.unsqueeze(2).to_broadcast([P, NJ, n]), C[tt].unsqueeze(1).to_broadcast([P, NJ, n]), ALU.mult))
                wrap(ssm_w[:, i, 0:NJ * n], ssm_w[:, i, 0:NJ * n], ssm_w[:, 4, 0:NJ * n])
                quarter(ssm_w[:, 2 + i, 0:NJ * n], ssm_w[:, i, 0:NJ * n], ssm_w[:, 4, 0:NJ * n])
            V.tensor_copy(R(25), R(9)).then_inc(sem("angles_ready"), 1)
            dve.wait_ge(sem("tables_ready"), 6)
            do(TT(R(10), R(10), R(4), ALU.mult))
            do(TT(R(11), R(11), R(4), ALU.mult))
            do(TS(R(10), R(10), -1.0, None, ALU.add))
            do(TT(R(13), lr, lr, ALU.mult))
            do(TT(R(14), li, li, ALU.mult))
            do(TT(R(13), R(13), R(14), ALU.add))
            do(V.reciprocal(R(13), R(13)))
            for dst, x, y, op in ((15, 10, 11, ALU.add), (16, 11, 10, ALU.subtract)):
                do(TT(R(14), R(x), lr, ALU.mult))
                do(TT(R(17), R(y), li, ALU.mult))
                do(TT(R(14), R(14), R(17), op))
                do(TT(R(dst), R(14), R(13), ALU.mult))
            dve.wait_ge(sem("b_loaded"), 32)
            dve.wait_ge(sem("blocks_zero"), 2)
            t0, t1 = (rot[:, 0, b, 0:256].rearrange("p (j c) -> p j c", j=NJ) for b in range(2))
            for r, (x, y, op) in enumerate(((0, 1, ALU.subtract), (1, 0, ALU.add))):
                do(TT(t0, bld[:, x], R(15).unsqueeze(2).to_broadcast([P, NJ, SG]), ALU.mult))
                do(TT(t1, bld[:, y], R(16).unsqueeze(2).to_broadcast([P, NJ, SG]), ALU.mult))
                for g in range(2):
                    rg = slice(64 * g, 64 * g + 64)
                    do(TT(bbd[rg, r, :, g], t0[rg], t1[rg], op))
            V.tensor_copy(R(26), R(9)).then_inc(sem("bbd_ready"), 1)
            dve.wait_ge(sem("c_turned"), 1)
            for r in range(2):
                for g in range(2):
                    rg = slice(64 * g, 64 * g + 64)
                    src = PB[4 + r][rg, :].rearrange("p (j g c) -> p j g c", j=NJ, g=2)[:, :, g]
                    do(TS(cbd[rg, r, :, g], src, (1.0, -1.0)[r], None, ALU.mult))
            V.tensor_copy(R(27), R(9)).then_inc(sem("cbd_ready"), 1)

            def ssm(j):
                B = lambda n: ssm_w[:, n]
                cs, sn = rot[:, j % 2, 0], rot[:, j % 2, 1]
                br, bi = PB[4][:], PB[5][:]
                dve.wait_ge(sem("rot_ready"), j + 1)
                dve.wait_ge(sem("bu_done"), j + 1)
                TT(B(0), cs, br, ALU.mult).then_inc(sem("dve_step"), 1)
                TT(B(1), sn, bi, ALU.mult).then_inc(sem("dve_step"), 1)
                TT(B(2), cs, bi, ALU.mult).then_inc(sem("dve_step"), 1)
                ch.n += 3
                TT(B(3), sn, br, ALU.mult).then_inc(sem("bu_read"), 1)
                dve.wait_ge(ch.sem, ch.n)
                TT(B(0), B(0), B(1), ALU.add).then_inc(sem("dve_step"), 1)
                dve.wait_ge(sem("bu_read"), j + 1)
                TT(B(2), B(2), B(3), ALU.subtract).then_inc(sem("dve_step"), 1)
                ch.n += 2
                dve.wait_ge(ch.sem, ch.n - 1)
                mag = sm[:, 4, j:j + 1].to_broadcast([P, T])
                V.tensor_tensor_scan(B(1), mag, B(0), 0.0, ALU.mult, ALU.add).then_inc(sem("dve_step"), 1)
                dve.wait_ge(ch.sem, ch.n)
                V.tensor_tensor_scan(B(3), mag, B(2), 0.0, ALU.mult, ALU.add).then_inc(sem("dve_step"), 1)
                ch.n += 2
                if j >= 2:
                    dve.wait_ge(sem("y_done"), j - 1)
                dve.wait_ge(ch.sem, ch.n)
                so = 4 + 2 * (j % 2)
                TT(B(0), cs, B(1), ALU.mult).then_inc(sem("dve_step"), 1)
                TT(B(2), sn, B(3), ALU.mult).then_inc(sem("dve_step"), 1)
                ch.n += 2
                dve.wait_ge(ch.sem, ch.n)
                do(TT(B(so), B(0), B(2), ALU.subtract))
                TT(B(0), sn, B(1), ALU.mult).then_inc(sem("dve_step"), 1)
                TT(B(2), cs, B(3), ALU.mult).then_inc(sem("dve_step"), 1)
                ch.n += 2
                dve.wait_ge(ch.sem, ch.n)
                TT(B(so + 1), B(0), B(2), ALU.add).then_inc(sem("s_ready"), 1)
                dve.wait_ge(sem("s_ready"), j + 1)

            def gelu(q):
                dve.wait_ge(sem("y_done"), 4 * q + 4)
                STT(gelu_b[:, 0], U[:, q], col(0, 84 + q), PB[6 + q % 2][:], ALU.mult, ALU.add).then_inc(sem("y_read"), 1)
                dve.wait_ge(sem("y_read"), q + 1)
                do(TT(gelu_b[:, 1], gelu_b[:, 0], gelu_b[:, 0], ALU.mult))
                do(TS(gelu_b[:, 1], gelu_b[:, 1], 0.044715, 1.0, ALU.mult, ALU.add))
                TT(gelu_b[:, 1], gelu_b[:, 1], gelu_b[:, 0], ALU.mult).then_inc(sem("gelu_in"), 1)
                dve.wait_ge(sem("gelu_tanh"), q + 1)
                STT(U[:, q], gelu_b[:, 2], 1.0, gelu_b[:, 0], ALU.add, ALU.mult).then_inc(sem("z_ready"), 1)
                dve.wait_ge(sem("z_ready"), q + 1)

            def bank(g):
                dve.wait_ge(sem("group_done"), g + 1)
                return PB[g % 4]

            def conv(h, c):
                g = first_group[f"cv{h}"] + c
                ps = bank(g)
                evacuated(dve, first_group[f"cg{h}"] + c)
                STT(VT[:, c], ps[:], b_in_col(20 + 4 * h + c), VT[:, c], ALU.add, ALU.mult).then_inc(sem("dve_evac"), 1)
                evacuated(dve, g)
                do(TS(CT[:, c], VT[:, c], conv_w_col(2, 4 * h + c), conv_b_col(4 * h + c), ALU.mult, ALU.add))
                do(STT(CT[:, c, 1:T], VT[:, c, 0:T - 1], conv_w_col(1, 4 * h + c), CT[:, c, 1:T], ALU.mult, ALU.add))
                STT(CT[:, c, 2:T], VT[:, c, 0:T - 2], conv_w_col(0, 4 * h + c), CT[:, c, 2:T], ALU.mult, ALU.add).then_inc(
                    sem("conv_done"), 1)

            def conv_gate(h, c):
                g = first_group[f"bg{h}"] + c
                ps = bank(g)
                dve.wait_ge(sem("conv_done"), 4 * h + c + 1)
                STT(YB[:, 4 * h + c], ps[:], b_in_col(4 + 4 * h + c), CT[:, c], ALU.add, ALU.mult).then_inc(sem("dve_evac"), 1)

            j = 0
            for name in ("cg0", "cv0", "bg0", "cg1", "cv1", "bg1", "gc0", "gc1"):
                for m in range(0, 4, 2):
                    for c in (m, m + 1):
                        if name[:2] == "cv":
                            conv(int(name[2]), c)
                        if name[:2] == "bg":
                            conv_gate(int(name[2]), c)
                    ssm(j)
                    if j in (6, 10, 14):
                        gelu((j - 6) // 4)
                    j += 1
            for h in range(2):
                for c in range(4):
                    g = first_group[f"co{h}"] + c
                    ps = bank(g)
                    evacuated(dve, first_group[f"gc{h}"] + c)
                    STT(GC[:, 4 * h + c], GC[:, 4 * h + c], 1.0, ps[:], ALU.add, ALU.mult).then_inc(sem("dve_evac"), 1)
                if h == 0:
                    gelu(3)
            g0 = first_group["gb"]
            for c in range(KD):
                ps = bank(g0 + 2 * c)
                evacuated(dve, g0 + 2 * c + 1)
                evacuated(dve, first_group[f"gs{c // 4}"] + c % 4)
                STT(at(112, 2), at(104 + 2 * (c % 2), 2), 1.0, ps[:], ALU.add, ALU.mult).then_inc(sem("dve_evac"), 1)
                evacuated(dve, g0 + 2 * c)
                do(STT(at(112, 2), YB[:, c], 1.0, at(112, 2), ALU.add, ALU.mult))
                STT(GC[:, c], GC[:, c], 4.0, at(112, 2), ALU.mult, ALU.add).then_inc(sem("merged"), 1)
                dve.wait_ge(sem("merged"), c + 1)
            V.tensor_copy(sc[:, 0], c1[:, 2, 0:16]).then_inc(sem("silu_in"), 1)
            dve.wait_ge(sem("x_back"), 16)
            for h in range(2):
                for k in range(KT):
                    ps = bank(first_group[f"wo{h}"] + k)
                    v = res[:, k, 512 * h:512 * h + 512]
                    STT(v, ps[:], 0.125, v, ALU.mult, ALU.add).then_inc(sem("dve_evac"), 1)
            unit_evacuated(dve, "wo1")
            dve.wait_ge(sem("silu_tanh"), 1)
            do(STT(sc[:, 0], sc[:, 1], 1.0, sc[:, 0], ALU.add, ALU.mult))
            do(TS(sc[:, 0], sc[:, 0], 0.5, None, ALU.mult))
            dve_rstd(dve, ch, KT, D, "n2")
            dve_scale_rows(dve, res, xn2, KT, "n2")

            def mod(m):
                name = f"mod{m}"
                loaded(dve, name)
                jobs = [(0, 512 * m)] + ([(8, 6144 + 512 * m)] if m < 4 else [])
                for k in range(KD):
                    for s, o in jobs:
                        acc = modacc[:, o:o + 512]
                        s_col = sc[:, 0, s + k:s + k + 1]
                        if k == 0:
                            ins = TS(acc, W[name][:, k], s_col, None, ALU.mult)
                        else:
                            ins = STT(acc, W[name][:, k], s_col, acc, ALU.mult, ALU.add)
                        if k == KD - 1 and s == jobs[-1][0]:
                            ins.then_inc(sem("mod_unit_used"), 1)
                            dve.wait_ge(sem("mod_unit_used"), m + 1)
                        else:
                            ch.n += 1
                            ins.then_inc(ch.sem, 1)
                    dve.wait_ge(ch.sem, ch.n)

            for name in names[names.index("f1_00"):]:
                if name[:3] == "mod":
                    mod(int(name[3:]))
                if name[:2] == "f2":
                    q = int(name[4])
                    for k in range(KT):
                        g = first_group[name] + k
                        ps = bank(g)
                        v = res[:, k, 256 * q:256 * q + 256]
                        TT(v, ps[:, 0:256], v, ALU.add).then_inc(sem("dve_evac"), 1)
                    if name == "f2_12":
                        dve_mod(dve, ch, do, bank)
            unit_evacuated(dve, "f2_13")
            dve_rstd(dve, ch, KT, D, "n3")
            dve.wait_ge(sem("gfb_loaded"), 16)
            for k in range(KT):
                STT(res[:, k], res[:, k], st[:, 4, k:k + 1], gfb, ALU.mult, ALU.mult).then_inc(sem("x1_ready"), 1)
                dve.wait_ge(sem("x1_ready"), k + 1)
            dve_second(dve, ch, do, bank)


        @block.gpsimd
        def _(pool):
            TT = nc.gpsimd.tensor_tensor
            pool.wait_ge(sem("tables_ready"), 6)
            pool.wait_ge(sem("c_turned"), 1)
            pool.wait_ge(sem("bbd_ready"), 1)
            pc = Count(sem("pool_step"))
            for j in range(NJ):
                """cos and sin of theta * (32 a + b), by the sums of their angles."""
                hi = lambda r: tab_h[:, r, j].unsqueeze(2).to_broadcast([P, 16, 32])
                lo = lambda r: tab_l[:, r, j].unsqueeze(1).to_broadcast([P, 16, 32])
                v = lambda x: x.rearrange("p (a b) -> p a b", a=16)
                t0, t1 = rot_t[:, 0], rot_t[:, 1]
                if j >= 2:
                    pool.wait_ge(sem("s_ready"), j - 1)
                for r, (x, y, op) in enumerate(((0, 1, ALU.subtract), (1, 0, ALU.add))):
                    pc.n += 1
                    TT(v(t0), hi(x), lo(0), ALU.mult).then_inc(pc.sem, 1)
                    pc.done(pool, TT(v(t1), hi(y), lo(1), ALU.mult))
                    ins = TT(rot[:, j % 2, r], t0, t1, op)
                    if r:
                        ins.then_inc(sem("rot_ready"), 1)
                        pool.wait_ge(sem("rot_ready"), j + 1)
                    else:
                        pc.done(pool, ins)
            pool_experts(pool)


_INS = ['x', 'norm_mix_g', 'w_in', 'b_in', 'lam_re', 'lam_im', 'log_dt', 'ssm_b_re', 'ssm_b_im', 'ssm_c_re',
        'ssm_c_im', 'ssm_d', 'w_glu_a', 'w_glu_b', 'conv_w', 'conv_b', 'w_conv_out', 'w_out', 'norm_mlp_g', 'w_ff1',
        'w_ff2', 'norm_final_g', 'c_2', 'ctx_2', 'c_ctx_2', 'w_mod_2', 'b_mod_2', 'norm1_g_2', 'w_in_2', 'conv_w_2',
        'a_log_2', 'dt_bias_2', 'onorm_g_2', 'w_out_2', 'norm2_g_2', 'w_group_2', 'b_group_2', 'w_router_2',
        'b_router_2', 'w_gate_2', 'w_up_2', 'w_down_2', 'final_g_2']


def kernel(**inputs):
    import concourse.bacc as _bacc
    from concourse.bass_utils import run_bass_kernel_spmd as _run

    nc = _bacc.Bacc("TRN2", target_bir_lowering=False, num_devices=1)
    values = {name: inputs[name] for name in _INS}
    values["consts"], values["dft_t"] = constants()
    arrays, args = {}, {}
    for name, value in values.items():
        value = np.ascontiguousarray(value)
        arrays[f"in_{name}_dram"] = value
        args[name] = nc.dram_tensor(f"in_{name}_dram", value.shape, mybir.dt.from_np(value.dtype),
                                    kind="ExternalInput").ap()
    out = nc.dram_tensor("out_0_dram", (1, T, D), F32, kind="ExternalOutput").ap()
    program(nc, args, out)
    r = _run(nc, [arrays], core_ids=[0])
    return r.results[0]["out_0_dram"]
```
